# Optimizing a Trainium2 kernel written in Bass

```python
import math
import jax
import jax.numpy as jnp
from jax import lax
import numpy as np

D_MODEL = 2048
BATCH = 1
SEQ = 512
DEPTH = 2

CHUNK = 64
N_MEM = 256
N_A_LAYERS = DEPTH // 2
N_B_LAYERS = DEPTH - N_A_LAYERS
MIX_WIDTH = D_MODEL
MAIN_WIDTH = 3 * MIX_WIDTH // 4
MEM_WIDTH = MIX_WIDTH - MAIN_WIDTH
HEAD_DIM = 128
SSM_GROUP = 16
SSM_GROUPS = MAIN_WIDTH // SSM_GROUP
SSM_STATE = 64
FOX_HEADS = MAIN_WIDTH // HEAD_DIM
MEM_HEADS = 4
MEM_HEAD_DIM = MEM_WIDTH // MEM_HEADS
Q_BLOCK = 128
IN_WIDTH = 2 * MAIN_WIDTH + 2 * MEM_WIDTH
EPS = 1e-6
DT_MIN = 1e-3
DT_MAX = 1e-1

kernel_name = "yoco_s5_fox_memory_hybrid"

def rmsnorm(x, g):
    xf = x.astype(jnp.float32)
    y = xf * lax.rsqrt(jnp.mean(xf * xf, axis=-1, keepdims=True) + EPS) * g.astype(jnp.float32)
    return y.astype(x.dtype)

def _scan_binop(e1, e2):
    a1r, a1i, b1r, b1i = e1
    a2r, a2i, b2r, b2i = e2
    ar = a2r * a1r - a2i * a1i
    ai = a2r * a1i + a2i * a1r
    br = a2r * b1r - a2i * b1i + b2r
    bi = a2r * b1i + a2i * b1r + b2i
    return (ar, ai, br, bi)

def s5_ssm(u, lam_re, lam_im, log_step, b_re, b_im, c_re, c_im, d_skip):
    bsz, seqlen, _ = u.shape
    uf = u.astype(jnp.float32)
    ug = uf.reshape(bsz, seqlen, SSM_GROUPS, SSM_GROUP)
    lr = lam_re.astype(jnp.float32)
    li = lam_im.astype(jnp.float32)
    dt = jnp.exp(log_step.astype(jnp.float32))[:, None]
    mag = jnp.exp(lr * dt)
    ar = mag * jnp.cos(li * dt)
    ai = mag * jnp.sin(li * dt)
    den = lr * lr + li * li
    cr = ((ar - 1.0) * lr + ai * li) / den
    ci = (ai * lr - (ar - 1.0) * li) / den
    br = b_re.astype(jnp.float32)
    bi = b_im.astype(jnp.float32)
    bbar_re = cr[..., None] * br - ci[..., None] * bi
    bbar_im = cr[..., None] * bi + ci[..., None] * br
    bu_re = jnp.einsum('blgh,gph->blgp', ug, bbar_re)
    bu_im = jnp.einsum('blgh,gph->blgp', ug, bbar_im)
    a_re = jnp.broadcast_to(ar[None, None], (1, seqlen, SSM_GROUPS, SSM_STATE))
    a_im = jnp.broadcast_to(ai[None, None], (1, seqlen, SSM_GROUPS, SSM_STATE))
    _, _, x_re, x_im = lax.associative_scan(_scan_binop, (a_re, a_im, bu_re, bu_im), axis=1)
    y = (jnp.einsum('blgp,ghp->blgh', x_re, c_re.astype(jnp.float32))
         - jnp.einsum('blgp,ghp->blgh', x_im, c_im.astype(jnp.float32)))
    y = y.reshape(bsz, seqlen, MAIN_WIDTH) + d_skip.astype(jnp.float32) * uf
    return y.astype(u.dtype)

def memory_attention(qm, mem, mem_g, w_mem_kv):
    bsz, seqlen, _ = qm.shape
    memn = rmsnorm(mem, mem_g)
    kv = memn @ w_mem_kv
    km, vm = jnp.split(kv, 2, axis=-1)
    km = km.reshape(bsz, -1, MEM_HEADS, MEM_HEAD_DIM).astype(jnp.float32)
    vm = vm.reshape(bsz, -1, MEM_HEADS, MEM_HEAD_DIM).astype(jnp.float32)
    q = qm.reshape(bsz, seqlen, MEM_HEADS, MEM_HEAD_DIM).astype(jnp.float32) * (MEM_HEAD_DIM ** -0.5)
    s = jnp.einsum('blhd,bmhd->bhlm', q, km)
    p = jax.nn.softmax(s, axis=-1)
    o = jnp.einsum('bhlm,bmhd->blhd', p, vm)
    return o.reshape(bsz, seqlen, MEM_WIDTH).astype(qm.dtype)

def forgetting_attention(q, k, v, fcum):
    _, seqlen, _, dh = q.shape
    qf = q.astype(jnp.float32) * (dh ** -0.5)
    kf = k.astype(jnp.float32)
    vf = v.astype(jnp.float32)
    outs = []
    for blk in range(seqlen // Q_BLOCK):
        q0 = blk * Q_BLOCK
        q1 = q0 + Q_BLOCK
        s = jnp.einsum('bqhd,bkhd->bhqk', qf[:, q0:q1], kf[:, :q1])
        s = s + fcum[:, :, q0:q1, None] - fcum[:, :, None, :q1]
        causal = jnp.arange(q0, q1)[:, None] >= jnp.arange(q1)[None, :]
        s = jnp.where(causal, s, -jnp.inf)
        p = jax.nn.softmax(s, axis=-1)
        outs.append(jnp.einsum('bhqk,bkhd->bqhd', p, vf[:, :q1]))
    return jnp.concatenate(outs, axis=1).astype(q.dtype)

def setup_inputs(seed: int = 0) -> dict:
    key = jax.random.key(seed)
    ks = jax.random.split(key, 32)
    f32 = jnp.float32
    D = D_MODEL
    nrm = lambda k, shape, scale: jax.random.normal(k, shape, f32) * scale
    x = jax.random.normal(ks[0], (BATCH, SEQ, D), f32)
    mem = jax.random.normal(ks[1], (BATCH, N_MEM, D), f32)
    pre_norm_g = 1.0 + nrm(ks[2], (DEPTH, D), 0.02)
    post_norm_g = 1.0 + nrm(ks[3], (DEPTH, D), 0.02)
    w_in_a = nrm(ks[4], (N_A_LAYERS, D, IN_WIDTH), D ** -0.5)
    lam_re = -0.5 + nrm(ks[5], (N_A_LAYERS, SSM_GROUPS, SSM_STATE), 0.01)
    lam_im = (math.pi * jnp.arange(SSM_STATE, dtype=f32))[None, None, :] + nrm(ks[6], (N_A_LAYERS, SSM_GROUPS, SSM_STATE), 0.01)
    log_step = jax.random.uniform(ks[7], (N_A_LAYERS, SSM_GROUPS), f32, math.log(DT_MIN), math.log(DT_MAX))
    b_re = nrm(ks[8], (N_A_LAYERS, SSM_GROUPS, SSM_STATE, SSM_GROUP), (2.0 * SSM_GROUP) ** -0.5)
    b_im = nrm(ks[9], (N_A_LAYERS, SSM_GROUPS, SSM_STATE, SSM_GROUP), (2.0 * SSM_GROUP) ** -0.5)
    c_re = nrm(ks[10], (N_A_LAYERS, SSM_GROUPS, SSM_GROUP, SSM_STATE), (2.0 * SSM_STATE) ** -0.5)
    c_im = nrm(ks[11], (N_A_LAYERS, SSM_GROUPS, SSM_GROUP, SSM_STATE), (2.0 * SSM_STATE) ** -0.5)
    d_skip = nrm(ks[12], (N_A_LAYERS, MAIN_WIDTH), 1.0)
    w_glu = nrm(ks[13], (N_A_LAYERS, MAIN_WIDTH, MAIN_WIDTH), MAIN_WIDTH ** -0.5)
    b_glu = nrm(ks[14], (N_A_LAYERS, MAIN_WIDTH), 0.01)
    kv_norm_g = 1.0 + nrm(ks[15], (D,), 0.02)
    w_kv = nrm(ks[16], (D, 2 * MAIN_WIDTH), D ** -0.5)
    w_fgate = nrm(ks[17], (D, FOX_HEADS), D ** -0.5)
    b_fgate = nrm(ks[18], (FOX_HEADS,), 0.1)
    w_in_b = nrm(ks[19], (N_B_LAYERS, D, IN_WIDTH), D ** -0.5)
    mem_norm_g = 1.0 + nrm(ks[20], (DEPTH, D), 0.02)
    w_mem_kv = nrm(ks[21], (DEPTH, D, 2 * MEM_WIDTH), D ** -0.5)
    w_out = nrm(ks[22], (DEPTH, MIX_WIDTH, D), MIX_WIDTH ** -0.5)
    return {"x": x, "mem": mem, "pre_norm_g": pre_norm_g, "post_norm_g": post_norm_g,
            "w_in_a": w_in_a, "lam_re": lam_re, "lam_im": lam_im, "log_step": log_step,
            "b_re": b_re, "b_im": b_im, "c_re": c_re, "c_im": c_im, "d_skip": d_skip,
            "w_glu": w_glu, "b_glu": b_glu, "kv_norm_g": kv_norm_g, "w_kv": w_kv,
            "w_fgate": w_fgate, "b_fgate": b_fgate, "w_in_b": w_in_b,
            "mem_norm_g": mem_norm_g, "w_mem_kv": w_mem_kv, "w_out": w_out}

def reference(x, mem, pre_norm_g, post_norm_g, w_in_a, lam_re, lam_im, log_step,
              b_re, b_im, c_re, c_im, d_skip, w_glu, b_glu, kv_norm_g, w_kv,
              w_fgate, b_fgate, w_in_b, mem_norm_g, w_mem_kv, w_out):
    bsz, seqlen, _ = x.shape
    h = x
    k_sh = v_sh = fcum = None
    split_pts = [MAIN_WIDTH, 2 * MAIN_WIDTH, 2 * MAIN_WIDTH + MEM_WIDTH]
    for i in range(DEPTH):
        hn = rmsnorm(h, pre_norm_g[i])
        if i < N_A_LAYERS:
            la = i
            proj = hn @ w_in_a[la]
            u, z, qm, zm = jnp.split(proj, split_pts, axis=-1)
            y = s5_ssm(u, lam_re[la], lam_im[la], log_step[la], b_re[la], b_im[la],
                       c_re[la], c_im[la], d_skip[la])
            yg = jax.nn.gelu(y)
            y = yg * jax.nn.sigmoid(yg @ w_glu[la] + b_glu[la])
            main = y * jax.nn.silu(z)
        else:
            lb = i - N_A_LAYERS
            proj = hn @ w_in_b[lb]
            q, z, qm, zm = jnp.split(proj, split_pts, axis=-1)
            q = q.reshape(bsz, seqlen, FOX_HEADS, HEAD_DIM)
            att = forgetting_attention(q, k_sh, v_sh, fcum).reshape(bsz, seqlen, MAIN_WIDTH)
            main = att * jax.nn.silu(z)
        memo = memory_attention(qm, mem, mem_norm_g[i], w_mem_kv[i]) * jax.nn.silu(zm)
        o = jnp.concatenate([main, memo], axis=-1) @ w_out[i]
        h = h + rmsnorm(o, post_norm_g[i])
        if i == N_A_LAYERS - 1:
            kv_in = rmsnorm(h, kv_norm_g)
            kv = kv_in @ w_kv
            k_sh, v_sh = jnp.split(kv, 2, axis=-1)
            k_sh = k_sh.reshape(bsz, seqlen, FOX_HEADS, HEAD_DIM)
            v_sh = v_sh.reshape(bsz, seqlen, FOX_HEADS, HEAD_DIM)
            logf = jax.nn.log_sigmoid((kv_in @ w_fgate).astype(jnp.float32) + b_fgate.astype(jnp.float32))
            fcum = jnp.transpose(jnp.cumsum(logf, axis=1), (0, 2, 1))
    return h


_drawn_inputs = setup_inputs


def setup_inputs(seed=0):
    import zlib

    import numpy as np

    out = dict(_drawn_inputs(seed))
    spreads = {}
    factors = {'post_norm_g': 2.701,
     'lam_re': 200.0,
     'b_glu': 64.0,
     'kv_norm_g': 13.466,
     'b_fgate': 3.064,
     'mem_norm_g': 8.0,
     'lam_im': 64.0,
     'log_step': 64.0,
     'b_re': 64.0,
     'b_im': 64.0,
     'c_re': 64.0,
     'c_im': 64.0}
    for name, (base, spread) in spreads.items():
        noise = np.random.default_rng([zlib.crc32(name.encode()), seed]).standard_normal(out[name].shape)
        drawn = base * np.exp(spread * noise) if base else spread * noise
        out[name] = jnp.asarray(drawn.astype(out[name].dtype))
    for name, factor in factors.items():
        out[name] = (out[name] * factor).astype(out[name].dtype)
    return out
```

```python
from contextlib import ExitStack

import concourse.bass as bass
from concourse import mybir

P = 128
T = 512
D = 2048
KD = D // P
NM = 256
HEADS = 12
MEMH = 4
UNITS = HEADS + MEMH
GROUPS = 96
GB = 8
NB = GROUPS // GB
TC = 8
NC = T // TC
IN_T = 32
EPS = 1e-6
SCALE = P ** -0.5

N_MEM, N_INA, N_GLU, N_OUTA, N_KV, N_FG, N_INB, N_OUTB, N_BLOCKS = 0, 16, 48, 60, 76, 100, 101, 133, 149

C_PRE, C_POST, C_KVG, C_MEMG, C_BGLU, C_DSKIP, N_COLS = 0, 32, 64, 80, 112, 124, 136

F32 = mybir.dt.float32
F32R = mybir.dt.float32r
I32 = mybir.dt.int32
ALU = mybir.AluOpType
ACT = mybir.ActivationFunctionType
AX = mybir.AxisListType

MAGIC = 12582912.0
INV_2PI = 0.15915494309189535
PI2_A = 6.28125
PI2_B = 0.001934051513671875
PI2_C = 1.255665914356996e-06
PI = 3.1415925
TWO_PI = 6.283185
HALF_PI = 1.5707963
LOG2E = 1.4426950408889634
LN2_A = 0.693359375
LN2_B = -2.12194440e-4
GELU_C = 0.7978845608028654
MASKED = -3.0e38


def trunk(nc, x_t, mem_t, cols_d, bfg_d, lam_d, bc_d, w_mem, w_in_a, w_glu, w_out, w_kv, w_fg, w_in_b, out_t):
    with ExitStack() as ctx:
        def dram(name, shape):
            return nc.dram_tensor(name, shape, F32, kind="Internal").ap()

        def sem(name):
            return ctx.enter_context(nc.semaphore(name))

        def sb(name, shape, dt=F32, stack=ctx):
            return stack.enter_context(nc.sbuf_tensor(name, shape, dt))

        proj_a = dram("proj_a", (IN_T, P, T))
        proj_b = dram("proj_b", (UNITS, P, T))
        y_s = dram("y_s", (NB, GB, P, NC))
        kv_s = dram("kv_s", (2 * HEADS, P, T))
        mem_s = dram("mem_s", (4 * MEMH, P, NM))
        lag_s = dram("lag_s", (2, P, (2 * TC - 1) * 16))
        fc_s = dram("fc_s", (HEADS, T))
        h_s = dram("h_s", (KD, P, T))

        raw = [sb(f"raw{i}", [P, KD * P]) for i in range(2)]
        w_hi = [sb(f"w_hi{i}", [P, KD, P], F32R) for i in range(2)]
        w_lo = [sb(f"w_lo{i}", [P, KD, P], F32R) for i in range(2)]
        act_hi = sb("act_hi", [P, KD, T], F32R)
        act_lo = sb("act_lo", [P, KD, T], F32R)
        stage = sb("stage", [P, 2, T])
        rbc = sb("rbc", [P, T])
        ident = sb("ident", [P, P])
        ones = sb("ones", [P, P])
        cols = sb("cols", [P, N_COLS])
        hbglu = sb("hbglu", [P, HEADS])
        consts = sb("consts", [P, 4])
        c_half_pi, c_sgn, c_nsgn, c_one = (consts[:, i:i + 1] for i in range(4))

        mask = sb("mask", [P, P])
        nmax = sb("nmax", [P, 4])
        rsum = sb("rsum", [P, 4])

        def overlay(specs):
            with ExitStack() as s:
                return [sb(name, shape, dt, s) for name, shape, dt in specs]

        mact_hi, mact_lo, acc0, sq0, var0, dev0, xs, vt0, rmem = overlay([
            ("mact_hi", [P, 2, KD, NM], F32R), ("mact_lo", [P, 2, KD, NM], F32R),
            ("acc0", [P, T], F32), ("sq0", [P, 2, T], F32), ("var0", [P, T], F32), ("dev0", [P, T], F32),
            ("xs", [P, 2, 2 * T], F32), ("vt0", [P, 2, T], F32), ("rmem", [P, NM], F32)])
        (gst, hc, hrot, g1, g2, toep, ublk, x1, x2, cos_t, sin_t, decay, tA, tB, up_re, up_im,
         dn_re, dn_im, bcp, bbar, bdiag, lagpad, ystage, omega8, mag8, cidx, bco) = overlay([
            ("gst", [P, GB, 16, TC], F32), ("hc", [P, 2, GB, TC + 1, 16], F32),
            ("hrot", [P, 2, GB, TC, 16], F32),
            ("g1", [P, GB, P], F32), ("g2", [P, GB, P], F32), ("toep", [P, 2, GB, P], F32),
            ("ublk", [P, 2, GB, NC], F32), ("x1", [P, GB, NC], F32), ("x2", [P, GB, NC], F32),
            ("cos_t", [P, T], F32), ("sin_t", [P, T], F32), ("decay", [P, T], F32),
            ("tA", [P, GB * 16 * (TC + 1)], F32), ("tB", [P, T], F32),
            ("up_re", [P, GROUPS, TC + 1], F32), ("up_im", [P, GROUPS, TC + 1], F32),
            ("dn_re", [P, GROUPS, TC], F32), ("dn_im", [P, GROUPS, TC], F32),
            ("bcp", [P, 4, P], F32), ("bbar", [P, 4, P], F32), ("bdiag", [P, GB * (P + 16)], F32),
            ("lagpad", [P, 2 * TC - 1, 16], F32), ("ystage", [P, T], F32),
            ("omega8", [P, GROUPS], F32), ("mag8", [P, GROUPS], F32),
            ("cidx", [P, NC], F32), ("bco", [P, 4, GROUPS], F32)])
        yg_hi, yg_lo, ym, um, yv, yq, yth = overlay([
            ("yg_hi", [P, HEADS, T], F32R), ("yg_lo", [P, HEADS, T], F32R),
            ("ym", [P, 2, T], F32), ("um", [P, 2, T], F32), ("yv", [P, 2, T], F32), ("yq", [P, 2, T], F32),
            ("yth", [P, 2, T], F32)])
        (_, q_a, k_a, v_a, s_a, p_a, z_a, zm_a, tz_a, tg_a, y2_a, sz_a) = overlay([
            ("under_yg", [P, 2, HEADS, T], F32),
            ("q_a", [P, MEMH, T], F32), ("k_a", [P, MEMH, NM], F32), ("v_a", [P, MEMH, NM], F32),
            ("s_a", [P, 4, NM], F32), ("p_a", [P, 2, T], F32), ("z_a", [P, 2, T], F32), ("zm_a", [P, T], F32),
            ("tz_a", [P, T], F32), ("tg_a", [P, T], F32), ("y2_a", [P, T], F32), ("sz_a", [P, T], F32)])
        o_t, h_t, vt1, acc1, sq1, var1, dev1, fga, fgb, fq = overlay([
            ("o_t", [P, KD, T], F32), ("h_t", [P, KD, T], F32), ("vt1", [P, 2, T], F32),
            ("acc1", [P, T], F32), ("sq1", [P, 2, T], F32), ("var1", [P, T], F32), ("dev1", [P, T], F32),
            ("fga", [P, T], F32), ("fgb", [P, T], F32), ("fq", [P, 4, HEADS], F32)])
        (s_b, pt_b, q_b, k_b, v_b, bias_b, cat_t, z_b, sz_b, _) = overlay([
            ("s_b", [P, 4, T], F32), ("pt_b", [P, 4, T], F32), ("q_b", [P, 2, T], F32), ("k_b", [P, 2, T], F32),
            ("v_b", [P, 2, T], F32), ("bias_b", [P, 2, T], F32), ("cat_t", [P, KD, T], F32),
            ("z_b", [P, 2, T], F32), ("sz_b", [P, 2, T], F32), ("tail", [P, 2, T], F32)])
        pgemm = ctx.enter_context(nc.psum_tensor("pgemm", [P, 2, T], F32))
        pt = ctx.enter_context(nc.psum_tensor("pt", [P, 2 * T], F32))
        ps = ctx.enter_context(nc.psum_tensor("ps", [P, 2, T], F32))
        p6 = ctx.enter_context(nc.psum_tensor("p6", [P, T], F32))
        p7 = ctx.enter_context(nc.psum_tensor("p7", [P, T], F32))

        raw_loaded = [sem("raw_loaded0"), sem("raw_loaded1")]
        hi_done, lo_done, gemm_done, out_taken = sem("hi_done"), sem("lo_done"), sem("gemm_done"), sem("out_taken")
        cols_loaded, consts_ready = sem("cols_loaded"), sem("consts_ready")
        xs_loaded = [sem("xs_loaded0"), sem("xs_loaded1")]
        act_hi_done, act_lo_done = sem("act_hi_done"), sem("act_lo_done")
        sq_ready, sq_used = sem("sq_ready"), sem("sq_used")
        stat_done, var_ready, dev_ready, r_ready = sem("stat_done"), sem("var_ready"), sem("dev_ready"), sem("r_ready")
        stage_stored = [sem("stage_stored0"), sem("stage_stored1")]
        vturned, vstaged = sem("vturned"), sem("vstaged")
        lam_loaded, sin_asked, sin_done = sem("lam_loaded"), sem("sin_asked"), sem("sin_done")
        region_clear = sem("region_clear")
        bc_loaded, toep_loaded = sem("bc_loaded"), [sem("toep_loaded0"), sem("toep_loaded1")]
        ublk_loaded = [sem("ublk_loaded0"), sem("ublk_loaded1")]
        params_ready, lags_done, g_ready, lag_stored = sem("params_ready"), sem("lags_done"), sem("g_ready"), sem("lag_stored")
        phase_ready, trig_done, states_done, rot_done = sem("phase_ready"), sem("trig_done"), sem("states_done"), sem("rot_done")
        ssm_y_done, y_taken, y_stored = sem("ssm_y_done"), sem("y_taken"), sem("y_stored")
        yu_loaded = [sem("yu_loaded0"), sem("yu_loaded1")]
        yv_ready, ysq_done, yin_ready, yth_done, yg_ready, yghi_done, yg_done = (
            sem(s) for s in ("yv_ready", "ysq_done", "yin_ready", "yth_done", "yg_ready", "yghi_done", "yg_done"))
        z_loaded = [sem("z_loaded0"), sem("z_loaded1")]
        zm_loaded, mq_loaded = sem("zm_loaded"), sem("mq_loaded")
        tz_done, main_ready = sem("tz_done"), sem("main_ready")
        qk_loaded = [sem("qk_loaded0"), sem("qk_loaded1")]
        v_loaded = [sem("v_loaded0"), sem("v_loaded1")]
        scores_done, max_ready, exp_done, probs_ready = (
            sem(s) for s in ("scores_done", "max_ready", "exp_done", "probs_ready"))
        turned, pt_ready, att_done, post_done, tanh_done = (
            sem(s) for s in ("turned", "pt_ready", "att_done", "post_done", "tanh_done"))
        p6_copied = sem("p6_copied")
        bfg_loaded, fg_ready, fg_exp, fg_ln_asked, fg_ln, fc_ready, fc_stored, fq_turned, fq_ready = (
            sem(s) for s in ("bfg_loaded", "fg_ready", "fg_exp", "fg_ln_asked", "fg_ln", "fc_ready", "fc_stored",
                             "fq_turned", "fq_ready"))
        x_loaded, h_ready, h_stored, h_loaded, out_stored = (
            sem(s) for s in ("x_loaded", "h_ready", "h_stored", "h_loaded", "out_stored"))
        dve_seq, act_seq = sem("dve_seq"), sem("act_seq")

        block = ctx.enter_context(nc.Block())

        def wait(e, s, value):
            if not isinstance(value, int) or value > 0:
                e.wait_ge(s, value)

        class Steps:

            def __init__(self, e, s):
                self.e, self.s, self.start, self.k = e, s, 0, 0

            def mark(self, ins):
                ins.then_inc(self.s, 1)
                self.k += 1

            def sync(self):
                self.e.wait_ge(self.s, self.start + self.k)

            def link(self, ins):
                self.mark(ins)
                self.sync()

            def loop(self, first, last, per, body):
                start = self.start + self.k
                with self.e.Fori(first, last - 1, 2) as i:
                    for j in (0, 1):
                        self.start, self.k = i * per + (start + (j - first) * per), 0
                        body(i + j, j)
                        assert self.k == per, (self.k, per)
                self.start, self.k = start + (last - first) * per, 0

        def pairs(e, first, last, body):
            with e.Fori(first, last - 1, 2) as i:
                for j in (0, 1):
                    body(i + j, j)

        def half(i, j):
            return (i - j) * 8 if not isinstance(i, int) else (i // 2) * 16

        def joined(u):
            return 3 + 2 * u

        def joined_main(g):
            return g + (min(max(g - 2, 0), MEMH) if isinstance(g, int) else MEMH)

        @block.sync
        def _(sp):
            def load(n, slot, src, width=KD * P):
                wait(sp, lo_done, n - 1)
                sp.dma_start(raw[slot][:, :width], src).then_inc(raw_loaded[slot], 16)

            def loads(base, first, last, src, width=KD * P):
                pairs(sp, first, last, lambda m, j: load(base + m, (base + j) % 2, src(m), width))

            for m in range(2):
                load(m, m, w_mem[m])
            loads(N_MEM, 2, 16, lambda m: w_mem[m])
            loads(N_INA, 0, 14, lambda m: w_in_a[m])

            def ublk_load(b, j):
                src = proj_a[b].rearrange("(g h) (t c) -> h t g c", g=GB, t=TC)
                sp.dma_start(ublk[:, j, :, :], src.rearrange("h t g c -> (h t) g c")).then_inc(ublk_loaded[j], 16)

            def batch_loads(b, j):
                sp.wait_ge(g_ready, b + 1)
                sp.dma_start(lag_s[j], lagpad[:].rearrange("p l h -> p (l h)")).then_inc(lag_stored, 16)
                sp.wait_ge(lag_stored, (b + 1) * 16)
                lag_rows = lag_s[j].rearrange("(g h) c -> h g c", g=GB)
                for t in range(TC):
                    sp.dma_start(toep[t:P:TC, j, :, :], lag_rows[:, :, (TC - 1 - t) * 16:(TC - 1 - t) * 16 + P]
                                 ).then_inc(toep_loaded[j], 16)

            sp.wait_ge(region_clear, 1)
            sp.wait_ge(stage_stored[0], 16 * 9)
            ublk_load(0, 0)

            def batch_step(b, j):
                last = isinstance(b, int) and b == 11
                if not last:
                    sp.wait_ge(params_ready, b + 1)
                    sp.dma_start(bcp[:, :, :], bc_d[b + 1]).then_inc(bc_loaded, 16)
                load(N_INA + 14 + b, j, w_in_a[14 + b])
                batch_loads(b, j)
                if last:
                    return
                wait(sp, ssm_y_done, b)
                sp.wait_ge(stage_stored[1 - j], b * 8 + 16 * 9 + 8 * j)
                ublk_load(b + 1, 1 - j)

            batch_step(0, 0)
            batch_step(1, 1)
            pairs(sp, 2, 10, batch_step)
            batch_step(10, 0)
            batch_step(11, 1)
            def yu_load(m, slot):
                for g in range(GB):
                    sp.dma_start(ym[16 * g:16 * g + 16, slot, :].rearrange("h (t c) -> h t c", t=TC),
                                 y_s[m, g].rearrange("(t h) c -> h t c", t=TC)).then_inc(yu_loaded[slot], 16)
                sp.dma_start(um[:, slot, :], proj_a[m]).then_inc(yu_loaded[slot], 16)

            load(N_INA + 26, 0, w_in_a[26])
            load(N_INA + 27, 1, w_in_a[27])
            sp.wait_ge(y_stored, 16 * NB)
            sp.wait_ge(rot_done, NB)
            yu_load(0, 0)
            yu_load(1, 1)

            def gelu_step(i, j, src, width=KD * P):
                load(N_INA + 28 + i, j, src, width)
                for slot in (0, 1):
                    sp.wait_ge(yv_ready, i * 2 + slot + 1)
                    yu_load(i * 2 + slot + 2, slot)

            pairs(sp, 0, 4, lambda i, j: gelu_step(i, j, w_in_a[28 + i]))
            gelu_step(4, 0, w_glu[0], HEADS * P)
            load(N_GLU + 1, 1, w_glu[1], HEADS * P)
            loads(N_GLU, 2, 12, lambda m: w_glu[m], HEADS * P)
            loads(N_OUTA, 0, 16, lambda m: w_out[0, m])
            loads(N_KV, 0, 24, lambda m: w_kv[m])
            load(N_FG, N_FG % 2, w_fg[0])

            loads(N_INB, 0, 16, lambda m: w_in_b[m])

            def qk_load(t, j, memory):
                wait(sp, scores_done, MEMH + t - 1)
                sp.dma_start(q_b[:, j, :], proj_b[t]).then_inc(qk_loaded[j], 16)
                if memory:
                    sp.dma_start(k_b[:, j, 0:NM], mem_s[t - HEADS + 2 * MEMH]).then_inc(qk_loaded[j], 16)
                else:
                    sp.dma_start(k_b[:, j, :], kv_s[t]).then_inc(qk_loaded[j], 16)
                    wait(sp, max_ready, MEMH + t - 1)
                    fc_row = fc_s[t:t + 1, :] if isinstance(t, int) else fc_s[bass.ds(t, 1), :]
                    sp.dma_start(bias_b[:, j, :], fc_row.partition_broadcast(P)).then_inc(qk_loaded[j], 16)

            def v_load(t, j, memory):
                wait(sp, att_done, MEMH + t - 1)
                if memory:
                    sp.dma_start(v_b[:, j, 0:NM], mem_s[t - HEADS + 3 * MEMH]).then_inc(v_loaded[j], 16)
                else:
                    sp.dma_start(v_b[:, j, :], kv_s[t + HEADS]).then_inc(v_loaded[j], 16)

            def unit_step(t, j, memory, memory_v):
                load(N_INB + 16 + t, (N_INB + j) % 2, w_in_b[16 + t])
                qk_load(t, j, memory)
                if not isinstance(t, int) or t >= 2:
                    v_load(t - 2, j, memory_v)

            sp.wait_ge(fc_stored, 16)
            sp.wait_ge(h_ready, 16)
            sp.wait_ge(stage_stored[0], 16 * 37)
            sp.wait_ge(stage_stored[1], 16 * 37)
            unit_step(0, 0, False, False)
            unit_step(1, 1, False, False)
            sp.wait_ge(stage_stored[0], 16 * 44)
            sp.wait_ge(stage_stored[1], 16 * 44)
            pairs(sp, 2, 12, lambda t, j: unit_step(t, j, False, False))
            unit_step(12, 0, True, False)
            unit_step(13, 1, True, False)
            unit_step(14, 0, True, True)
            unit_step(15, 1, True, True)
            load(N_OUTB, N_OUTB % 2, w_out[1, 0])
            v_load(14, 0, True)
            load(N_OUTB + 1, (N_OUTB + 1) % 2, w_out[1, 1])
            v_load(15, 1, True)
            loads(N_OUTB, 2, 16, lambda m: w_out[1, m])
            sp.wait_ge(act_lo_done, 96)
            sp.dma_start(h_t[:, :, :], h_s.rearrange("k p t -> p k t")).then_inc(h_loaded, 16)
            for k in range(0, KD, 4):
                sp.wait_ge(h_ready, 16 + k + 4)
                sp.dma_start(out_t[k:k + 4].rearrange("k p t -> p k t"), h_t[:, k:k + 4, :]).then_inc(out_stored, 16)
            sp.wait_ge(out_stored, 64)

        @block.gpsimd
        def _(pool):
            nc.gpsimd.memset(ones[:, :], 1.0).then_inc(consts_ready, 1)
            nc.gpsimd.memset(ident[:, :], 0.0).then_inc(consts_ready, 1)
            nc.gpsimd.memset(mask[:, :], 0.0).then_inc(consts_ready, 1)
            nc.gpsimd.memset(c_half_pi, HALF_PI).then_inc(consts_ready, 1)
            nc.gpsimd.memset(c_sgn, -1.0).then_inc(consts_ready, 1)
            nc.gpsimd.memset(c_nsgn, 1.0).then_inc(consts_ready, 1)
            nc.gpsimd.memset(c_one, 1.0).then_inc(consts_ready, 1)
            pool.wait_ge(consts_ready, 7)
            nc.gpsimd.memset(consts[64:P, 1:2], 1.0).then_inc(consts_ready, 1)
            nc.gpsimd.memset(consts[64:P, 2:3], -1.0).then_inc(consts_ready, 1)
            pool.wait_ge(consts_ready, 9)
            nc.gpsimd.affine_select(out=ident[:, :], in_=ident[:, :], compare_op=ALU.not_equal, fill=1.0, base=0,
                                    pattern=[[-1, P]], channel_multiplier=1).then_inc(consts_ready, 1)
            nc.gpsimd.affine_select(out=mask[:, :], in_=mask[:, :], compare_op=ALU.is_ge, fill=MASKED, base=0,
                                    pattern=[[-1, P]], channel_multiplier=1).then_inc(consts_ready, 1)

            def low(n, slot):
                pool.wait_ge(hi_done, n + 1)
                nc.gpsimd.tensor_tensor(w_lo[slot][:, :, :], raw[slot][:, :].rearrange("p (k m) -> p k m", k=KD),
                                        w_hi[slot][:, :, :].bitcast(F32), ALU.subtract).then_inc(lo_done, 1)

            pairs(pool, 0, 18, low)
            pool.wait_ge(gemm_done, 16)
            pool.wait_ge(vstaged, 8)
            pool.wait_ge(r_ready, 2)
            nc.gpsimd.memset(x1[:, :, :], 0.0)
            nc.gpsimd.memset(x2[:, :, :], 0.0)
            nc.gpsimd.memset(lagpad[:, :, :], 0.0)
            nc.gpsimd.memset(bdiag[:, :], 0.0)
            nc.gpsimd.iota(cidx[:, :], pattern=[[1, NC]], base=0, channel_multiplier=0,
                           allow_small_or_imprecise_dtypes=True).then_inc(region_clear, 1)
            pairs(pool, 18, N_KV + 2, low)

            pool.wait_ge(sq_ready, 49)
            nc.gpsimd.tensor_copy(acc1[:, :], sq1[:, 0, :]).then_inc(sq_used, 1)

            def total(k, slot):
                pool.wait_ge(sq_ready, 49 + k)
                pool.wait_ge(sq_used, 48 + k)
                nc.gpsimd.tensor_tensor(acc1[:, :], acc1[:, :], sq1[:, slot, :], ALU.add).then_inc(sq_used, 1)

            total(1, 1)
            pairs(pool, 2, 16, total)
            pairs(pool, N_KV + 2, N_BLOCKS - 1, low)
            low(N_BLOCKS - 1, (N_BLOCKS - 1) % 2)

        @block.tensor
        def _(pe):
            def gemm(n, slot, hi, lo, kt=KD, width=T, splits=None, order=None, split_done=act_lo_done, halfway=None):
                pe.wait_ge(hi_done, n + 1)
                pe.wait_ge(lo_done, n + 1)
                wait(pe, out_taken, n - 1)
                out = pgemm[:, slot, 0:width]
                for i, k in enumerate(order or range(kt)):
                    if splits is not None:
                        pe.wait_ge(split_done, splits + i + 1)
                    if i == kt // 2 and halfway is not None:
                        halfway()
                    pe.matmul(out, w_hi[slot][:, k, :], hi[:, k, :], start=(i == 0), stop=False)
                    pe.matmul(out, w_hi[slot][:, k, :], lo[:, k, :], start=False, stop=False)
                    last = pe.matmul(out, w_lo[slot][:, k, :], hi[:, k, :], start=False, stop=(i == kt - 1))
                last.then_inc(gemm_done, 1)

            def blocks(base, first, last, kt=KD, hi=act_hi, lo=act_lo):
                pairs(pe, first, last, lambda m, j: gemm(base + m, (base + j) % 2, hi, lo, kt))

            def stat(e, acc, width=T):
                pe.wait_ge(sq_used, 16 * (e + 1))
                pe.matmul(p7[:, 0:width], ones[:, :], acc[:, 0:width], start=True, stop=True).then_inc(stat_done, 1)

            def turn_values(c, n, vt, slot, tiles):
                pe.wait_ge(out_taken, n + 1)
                wait(pe, vstaged, c)
                for i in range(tiles):
                    last = pe.transpose(pt[:, i * P:(i + 1) * P], vt[:, slot, i * P:(i + 1) * P], ident[:, :])
                last.then_inc(vturned, 1)

            pe.wait_ge(consts_ready, 11)
            for layer in (0, 1):
                hi, lo = mact_hi[:, layer], mact_lo[:, layer]
                for r in range(2 * MEMH):
                    n = 8 * layer + r
                    gemm(n, n % 2, hi, lo, KD, NM, splits=0 if n == 0 else None)
                    if n == 0:
                        stat(0, acc0, NM)
                    if r > MEMH:
                        turn_values(4 * layer + r - 5, n - 1, vt0, (n - 1) % 2, 2)
                turn_values(4 * layer + 3, 8 * layer + 7, vt0, 1, 2)

            stat(1, acc0)
            gemm(N_INA, 0, act_hi, act_lo, splits=16)
            gemm(N_INA + 1, 1, act_hi, act_lo)
            blocks(N_INA, 2, 12)

            def group_params(b, j):
                pe.wait_ge(params_ready, b + 1)
                wait(pe, g_ready, b)
                for g in range(GB):
                    pe.transpose(pt[:, g * P:(g + 1) * P], gst[:, g, :, :].rearrange("p h t -> p (h t)"), ident[:, :])
                for g in range(GB):
                    last = pe.matmul(p7[:, 0:P], bdiag[:, g * P:(g + 1) * P],
                                     hc[:, j, g, 0:TC, :].rearrange("p l h -> p (l h)"),
                                     start=(g == 0), stop=(g == GB - 1))
                last.then_inc(lags_done, 1)

            def group_states(b, j):
                pe.wait_ge(g_ready, b + 1)
                pe.wait_ge(ublk_loaded[j], half(b, j) + 16)
                wait(pe, rot_done, b)
                for g in range(GB):
                    cols_g = slice(g * NC, (g + 1) * NC)
                    pe.matmul(ps[:, 0, cols_g], g1[:, g, :], ublk[:, j, g, :], start=True, stop=True)
                    last = pe.matmul(ps[:, 1, cols_g], g2[:, g, :], ublk[:, j, g, :], start=True, stop=True)
                last.then_inc(states_done, 1)

            def group_outputs(b, j):
                pe.wait_ge(rot_done, b + 1)
                pe.wait_ge(toep_loaded[j], (half(b, j) + 16) * TC)
                wait(pe, y_taken, b)
                for g in range(GB):
                    out = p6[:, g * NC:(g + 1) * NC]
                    pe.matmul(out, toep[:, j, g, :], ublk[:, j, g, :], start=True, stop=False)
                    pe.matmul(out, hc[:, j, g, 1:TC + 1, :].rearrange("p l h -> p (l h)"), x1[:, g, :],
                              start=False, stop=False)
                    last = pe.matmul(out, hrot[:, j, g, :, :].rearrange("p l h -> p (l h)"), x2[:, g, :],
                                     start=False, stop=True)
                last.then_inc(ssm_y_done, 1)

            def batch(b, j):
                group_params(b, j)
                before = not isinstance(b, int) or b > 0
                gemm(N_INA + 12 + b, j, act_hi, act_lo,
                     halfway=(lambda: group_outputs(b - 1, 1 - j)) if before else None)
                group_states(b, j)

            batch(0, 0)
            batch(1, 1)
            pairs(pe, 2, 12, batch)
            gemm(N_INA + 24, 0, act_hi, act_lo, halfway=lambda: group_outputs(11, 1))
            gemm(N_INA + 25, 1, act_hi, act_lo)
            blocks(N_INA, 26, 32)

            def mem_scores(u, q, k):
                wait(pe, max_ready, u)
                for i in range(4):
                    last = pe.matmul(ps[:, i // 2, (i % 2) * NM:(i % 2 + 1) * NM], q[:, i * P:(i + 1) * P], k,
                                     start=(i % 2 == 0), stop=True, skip_group_check=True)
                last.then_inc(scores_done, 1)

            def mem_turn(u, s):
                pe.wait_ge(probs_ready, u + 1)
                wait(pe, pt_ready, u)
                for m in range(2):
                    for i in range(4):
                        last = pe.transpose(pt[:, m * T + i * P:m * T + (i + 1) * P], s[:, i, m * P:(m + 1) * P],
                                            ident[:, :])
                last.then_inc(turned, 1)

            def mem_values(u, v, p_t):
                pe.wait_ge(pt_ready, u + 1)
                for m in range(2):
                    last = pe.matmul(p7[:, :], v[:, m * P:(m + 1) * P], p_t[:, m, :], start=(m == 0), stop=(m == 1))
                last.then_inc(att_done, 1)

            def gate(g):
                gemm(N_GLU + g, g % 2, yg_hi, yg_lo, HEADS)

            gemm(N_GLU, 0, yg_hi, yg_lo, HEADS, splits=0, split_done=yg_done)
            pe.wait_ge(mq_loaded, 48)
            for u in range(MEMH + 1):
                if u < MEMH:
                    mem_scores(u, q_a[:, u, :], k_a[:, u, :])
                gate(u + 1)
                if u > 0:
                    if u > 1:
                        pe.wait_ge(main_ready, joined(u - 2) + 1)
                    mem_values(u - 1, v_a[:, u - 1, :], p_a)
                if u < MEMH:
                    mem_turn(u, s_a)
            blocks(N_GLU, 6, 12, HEADS, yg_hi, yg_lo)

            made = sorted(range(KD), key=lambda k: joined_main(k) if k < HEADS else joined(k - HEADS))
            gemm(N_OUTA, 0, act_hi, act_lo, splits=32, order=made)
            gemm(N_OUTA + 1, 1, act_hi, act_lo)
            blocks(N_OUTA, 2, 16)
            stat(2, acc1)
            gemm(N_KV, 0, act_hi, act_lo, splits=48)
            stat(3, acc1)
            gemm(N_KV + 1, 1, act_hi, act_lo)
            blocks(N_KV, 2, 12)
            gemm(N_KV + 12, 0, act_hi, act_lo)
            gemm(N_KV + 13, 1, act_hi, act_lo)
            turn_values(8, N_KV + 12, vt1, 0, 4)

            def value_block(m, j):
                gemm(N_KV + 12 + m, j, act_hi, act_lo)
                turn_values(m + 7, N_KV + 11 + m, vt1, 1 - j, 4)

            pairs(pe, 2, 12, value_block)
            turn_values(19, N_KV + 23, vt1, 1, 4)
            gemm(N_FG, N_FG % 2, act_hi, act_lo)

            gemm(N_INB, 1, act_hi, act_lo, splits=64)
            pe.wait_ge(fc_ready, 1)
            pe.wait_ge(vstaged, 20)
            for i in range(4):
                last = pe.transpose(pt[:, i * HEADS:(i + 1) * HEADS], fgb[0:HEADS, i * P:(i + 1) * P],
                                    ident[0:HEADS, 0:HEADS])
            last.then_inc(fq_turned, 1)
            gemm(N_INB + 1, 0, act_hi, act_lo)
            blocks(N_INB, 2, 16)

            def fox_scores(t, j):
                wait(pe, max_ready, MEMH + t)
                q, k = q_b[:, j, :], k_b[:, j, :]
                first = dict(start=True, stop=True, skip_group_check=True)
                more = dict(start=False, stop=True, skip_group_check=True)
                pe.matmul(ps[:, 0, 0:P], q[:, 0:P], k[:, 0:P], **first)
                pe.matmul(ps[:, 0, P:4 * P], q[:, 2 * P:3 * P], k[:, 0:3 * P], **more)
                pe.matmul(ps[:, 1, :], q[:, 3 * P:4 * P], k, **first)
                wait(pe, p6_copied, t)
                pe.matmul(p6[:, 0:2 * P], q[:, P:2 * P], k[:, 0:2 * P], **first).then_inc(scores_done, 1)

            def fox_turn(t):
                pe.wait_ge(probs_ready, MEMH + t + 1)
                pe.wait_ge(pt_ready, MEMH + t)
                for i, out in ((3, pt[:, 0:T]), (2, pt[:, T:T + 3 * P]), (0, pt[:, T + 3 * P:2 * T]), (1, p6[:, 2 * P:T])):
                    for k in range(i + 1):
                        last = pe.transpose(out[:, k * P:(k + 1) * P], s_b[:, i, k * P:(k + 1) * P], ident[:, :])
                last.then_inc(turned, 1)

            def fox_values(t, j):
                pe.wait_ge(pt_ready, MEMH + t + 1)
                pe.wait_ge(v_loaded[j], half(t, j) + 16)
                wait(pe, post_done, t)
                for k in range(4):
                    last = pe.matmul(p7[:, k * P:T], v_b[:, j, k * P:(k + 1) * P], pt_b[:, k, k * P:T],
                                     start=(k == 0), stop=(k == 3), skip_group_check=True)
                last.then_inc(att_done, 1)

            def fox(t, j):
                pe.wait_ge(qk_loaded[j], half(t, j) * 3 + 48)
                fox_scores(t, j)
                gemm(N_INB + 16 + t, (N_INB + j) % 2, act_hi, act_lo)
                if not isinstance(t, int) or t > 0:
                    fox_values(t - 1, 1 - j)
                fox_turn(t)

            fox(0, 0)
            fox(1, 1)
            pairs(pe, 2, 12, fox)
            for t in range(HEADS, UNITS):
                j = t % 2
                pe.wait_ge(qk_loaded[j], 16 * (18 + 2 * ((t - HEADS) // 2 + 1)))
                mem_scores(MEMH + t, q_b[:, j, :], k_b[:, j, 0:NM])
                gemm(N_INB + 16 + t, (N_INB + j) % 2, act_hi, act_lo)
                if t == HEADS:
                    fox_values(t - 1, 1 - j)
                else:
                    pe.wait_ge(v_loaded[1 - j], 16 * ((t - 1) // 2 + 1))
                    pe.wait_ge(post_done, t - 1)
                    mem_values(MEMH + t - 1, v_b[:, 1 - j, :], pt_b)
                mem_turn(MEMH + t, s_b)
            pe.wait_ge(v_loaded[1], 16 * 8)
            pe.wait_ge(post_done, UNITS - 1)
            mem_values(MEMH + 15, v_b[:, 1, :], pt_b)

            gemm(N_OUTB, 1, act_hi, act_lo, splits=80)
            gemm(N_OUTB + 1, 0, act_hi, act_lo)
            blocks(N_OUTB, 2, 16)
            stat(4, acc1)

        @block.scalar
        def _(act):
            def high(n, slot):
                wait(act, gemm_done, n - 1)
                act.wait_ge(raw_loaded[slot], half(n, slot) + 16)
                act.activation(w_hi[slot][:, :, :], raw[slot][:, :].rearrange("p (k m) -> p k m", k=KD),
                               ACT.Copy).then_inc(hi_done, 1)

            def store(n, s, slot, dst):
                act.wait_ge(out_taken, n + 1)
                act.dma_start(dst, stage[:, slot, :]).then_inc(stage_stored[slot], 16)

            def value_out(c, s, slot, width, dst):
                act.wait_ge(vturned, c + 1)
                wait(act, stage_stored[slot], half(s, slot))
                act.activation(stage[:, slot, 0:width], pt[:, 0:width], ACT.Copy).then_inc(vstaged, 1)
                act.wait_ge(vstaged, c + 1)
                act.dma_start(dst, stage[:, slot, 0:width]).then_inc(stage_stored[slot], 16)

            def square(q, slot, src, sq):
                wait(act, sq_used, q - 1)
                act.activation(sq[:, slot, 0:src.shape[-1]], src, ACT.Square).then_inc(sq_ready, 1)

            def deviation(e, var, dev, width=T):
                act.wait_ge(var_ready, e + 1)
                act.activation(dev[:, 0:width], var[:, 0:width], ACT.Sqrt).then_inc(dev_ready, 1)

            act.dma_start(cols[:, :], cols_d).then_inc(cols_loaded, 16)

            def mem_load(g):
                act.dma_start(xs[:, g % 2, :].rearrange("p (k t) -> p k t", k=4),
                              mem_t[4 * g:4 * g + 4].rearrange("k p t -> p k t")).then_inc(xs_loaded[g % 2], 16)

            def x_load(k, slot):
                act.dma_start(xs[:, slot, 0:T], x_t[k]).then_inc(xs_loaded[slot], 16)

            mem_load(0)
            mem_load(1)
            act.wait_ge(cols_loaded, 16)
            for g in range(4):
                act.wait_ge(xs_loaded[g % 2], 16 * (g // 2 + 1))
                for k in range(4 * g, 4 * g + 4):
                    src = xs[:, g % 2, (k % 4) * NM:(k % 4 + 1) * NM]
                    for layer in (0, 1):
                        c = C_MEMG + layer * KD + k
                        act.activation(mact_hi[:, layer, k, :], src, ACT.Identity,
                                       scale=cols[:, c:c + 1]).then_inc(act_hi_done if layer else act_seq, 1)
                    square(k, k % 2, src, sq0)
                    if k == 1:
                        high(0, 0)
                    if k == 5:
                        high(1, 1)
                act.wait_ge(sq_ready, 4 * g + 4)
                act.wait_ge(act_lo_done, 4 * g + 4)
                if g < 2:
                    mem_load(g + 2)
                else:
                    x_load(g - 2, g - 2)

            def x_tile(k, slot):
                act.wait_ge(xs_loaded[slot], half(k, slot) + 48)
                act.activation(act_hi[:, k, :], xs[:, slot, 0:T], ACT.Identity,
                               scale=cols[:, bass.ds(C_PRE + k, 1)]).then_inc(act_hi_done, 1)
                square(16 + k, slot, xs[:, slot, 0:T], sq0)
                if not isinstance(k, int) or k < 14:
                    act.wait_ge(sq_ready, 17 + k)
                    act.wait_ge(act_lo_done, 17 + k)
                    x_load(k + 2, slot)

            for n in range(16):
                if n == 0:
                    deviation(0, var0, dev0, NM)
                high(n + 2, n % 2)
                x_tile(n, n % 2)
                r = n % 8
                if r < MEMH:
                    act.wait_ge(out_taken, n + 1)
                    act.dma_start(mem_s[n], stage[:, n % 2, 0:NM]).then_inc(stage_stored[n % 2], 16)
                elif r > MEMH:
                    value_out(4 * (n // 8) + r - 5, n - 1, (n - 1) % 2, NM, mem_s[n - 1])
                if r == 7:
                    value_out(4 * (n // 8) + 3, n, n % 2, NM, mem_s[n])

            deviation(1, var0, dev0)

            def u_block(m, j):
                high(N_INA + m + 2, j)
                store(N_INA + m, 16 + m, j, proj_a[m])

            u_block(0, 0)
            u_block(1, 1)
            act.wait_ge(region_clear, 1)
            act.dma_start(tB[:, 0:3 * GROUPS], lam_d).then_inc(lam_loaded, 16)
            act.dma_start(bcp[:, :, :], bc_d[0]).then_inc(bc_loaded, 16)
            pairs(act, 2, 4, u_block)
            act.wait_ge(sin_asked, 1)
            act.activation(bco[:, 0, :], bco[:, 0, :], ACT.Sin).then_inc(sin_done, 1)
            act.activation(bco[:, 1, :], bco[:, 1, :], ACT.Sin, scale=0.5).then_inc(sin_done, 1)
            pairs(act, 4, 12, u_block)

            def batch(b, j):
                act.wait_ge(phase_ready, b + 1)
                act.activation(sin_t[:, :], tB[:, :], ACT.Sin, scale=-TWO_PI)
                act.activation(cos_t[:, :], tA[:, 0:T], ACT.Sin, scale=-TWO_PI, bias=c_half_pi).then_inc(trig_done, 1)
                act.wait_ge(lags_done, b + 1)
                wait(act, states_done, b)
                wait(act, lag_stored, b * 16)
                ptg = pt[:, :].rearrange("p (g s) -> p g s", g=GB)
                act.activation(g1[:, :, :], ptg, ACT.Copy)
                act.activation(g2[:, :, 0:64], ptg[:, :, 64:P], ACT.Copy)
                act.activation(g2[:, :, 64:P], ptg[:, :, 0:64], ACT.Copy, scale=-1.0)
                act.activation(lagpad[:, TC - 1:, :], p7[:, 0:P].rearrange("p (l h) -> p l h", l=TC),
                               ACT.Copy).then_inc(g_ready, 1)
                if not isinstance(b, int) or b > 0:
                    y_out(b - 1)
                high(N_INA + 14 + b, j)
                store(N_INA + 12 + b, 28 + b, j, proj_a[12 + b])

            def y_out(b):
                act.wait_ge(ssm_y_done, b + 1)
                wait(act, y_stored, b * 16)
                act.activation(ystage[:, :], p6[:, :], ACT.Copy).then_inc(y_taken, 1)
                act.wait_ge(y_taken, b + 1)
                act.dma_start(y_s[b].rearrange("g q c -> q g c"),
                              ystage[:, :].rearrange("p (g c) -> p g c", g=GB)).then_inc(y_stored, 16)

            batch(0, 0)
            batch(1, 1)
            pairs(act, 2, 12, batch)
            high(N_INA + 26, 0)
            store(N_INA + 24, 40, 0, proj_a[24])
            y_out(11)
            high(N_INA + 27, 1)
            store(N_INA + 25, 41, 1, proj_a[25])

            def gelu_block(i, j):
                for slot in (0, 1):
                    m = i * 2 + slot
                    act.wait_ge(yv_ready, m + 1)
                    act.activation(yq[:, slot, :], yv[:, slot, :], ACT.Square).then_inc(ysq_done, 1)
                for slot in (0, 1):
                    act.wait_ge(yin_ready, i * 2 + slot + 1)
                    act.activation(yth[:, slot, :], yq[:, slot, :], ACT.Tanh, scale=GELU_C).then_inc(yth_done, 1)
                for slot in (0, 1):
                    m = i * 2 + slot
                    act.wait_ge(yg_ready, m + 1)
                    act.activation(yg_hi[:, m, :], yv[:, slot, :], ACT.Copy, scale=0.5).then_inc(yghi_done, 1)
                high(N_INA + 28 + i, j)
                store(N_INA + 26 + i, 42 + i, j, proj_a[26 + i])

            pairs(act, 0, 6, gelu_block)

            def exps(u, s, widths, tile):
                act.wait_ge(max_ready, u + 1)
                for i, w in enumerate(widths):
                    last = act.activation(s[:, i, 0:w], s[:, i, 0:w] if tile is None else tile(i), ACT.Exp,
                                          bias=nmax[:, i:i + 1], accum_out=rsum[:, i:i + 1])
                last.then_inc(exp_done, 1)

            def mem_pt(u, p_t):
                act.wait_ge(turned, u + 1)
                wait(act, att_done, u)
                for m in range(2):
                    last = act.activation(p_t[:, m, :], pt[:, m * T:(m + 1) * T], ACT.Copy)
                last.then_inc(pt_ready, 1)

            def z_load(g, slot):
                act.dma_start(z_a[:, slot, :], proj_a[12 + g]).then_inc(z_loaded[slot], 16)

            def zm_load(u):
                act.dma_start(zm_a[:, :], proj_a[28 + u]).then_inc(zm_loaded, 16)

            def gate_block(g, j, last_two=False):
                n, c = N_GLU + g, joined_main(g)
                unit = g - 1 if isinstance(g, int) and 1 <= g <= MEMH else None
                after = g - 2 if isinstance(g, int) and 2 <= g <= MEMH + 1 else None
                if unit is not None:
                    exps(unit, s_a, [NM] * 4, None)
                wait(act, main_ready, c)
                act.wait_ge(z_loaded[j], half(g, j) + 16)
                act.activation(tz_a[:, :], z_a[:, j, :], ACT.Tanh, scale=0.5).then_inc(tz_done, 1)
                act.wait_ge(gemm_done, n + 1)
                act.activation(tg_a[:, :], pgemm[:, j, :], ACT.Tanh, scale=0.5,
                               bias=hbglu[:, bass.ds(g, 1)]).then_inc(out_taken, 1)
                high(n + 2, j)
                act.wait_ge(main_ready, c + 1)
                act.activation(act_hi[:, g, :], y2_a[:, :], ACT.Copy, scale=0.25).then_inc(act_hi_done, 1)
                if not last_two:
                    z_load(g + 2, j)
                if unit is not None:
                    mem_pt(unit, p_a)
                if after is not None:
                    act.wait_ge(zm_loaded, 16 * (after + 1))
                    act.activation(tz_a[:, :], zm_a[:, :], ACT.Tanh, scale=0.5).then_inc(tz_done, 1)
                    act.wait_ge(main_ready, c + 2)
                    act.activation(act_hi[:, HEADS + after, :], y2_a[:, :], ACT.Copy, scale=0.5).then_inc(act_hi_done, 1)
                    if after < MEMH - 1:
                        zm_load(after + 1)

            act.wait_ge(yg_done, HEADS)
            z_load(0, 0)
            z_load(1, 1)
            act.wait_ge(stage_stored[0], 16 * 24)
            act.wait_ge(stage_stored[1], 16 * 24)
            act.dma_start(q_a[:, :, :], proj_a[24:28].rearrange("k p t -> p k t")).then_inc(mq_loaded, 16)
            act.dma_start(k_a[:, :, :], mem_s[0:4].rearrange("k p t -> p k t")).then_inc(mq_loaded, 16)
            act.dma_start(v_a[:, :, :], mem_s[4:8].rearrange("k p t -> p k t")).then_inc(mq_loaded, 16)
            zm_load(0)
            for g in range(6):
                gate_block(g, g % 2)
            pairs(act, 6, 10, gate_block)
            gate_block(10, 0, True)
            gate_block(11, 1, True)

            act.wait_ge(act_lo_done, 48)
            act.wait_ge(gemm_done, N_OUTA)
            act.dma_start(h_t[:, :, :], x_t.rearrange("k p t -> p k t")).then_inc(x_loaded, 16)

            def out_block(base, q):
                def body(m, j, more=True):
                    slot = (base + j) % 2
                    if more:
                        high(base + m + 2, slot)
                    act.wait_ge(gemm_done, base + m + 1)
                    square(q + m, j, pgemm[:, slot, :], sq1)
                    act.activation(o_t[:, m, :], pgemm[:, slot, :], ACT.Copy).then_inc(out_taken, 1)
                return body

            pairs(act, 0, 16, out_block(N_OUTA, 32))
            deviation(2, var1, dev1)

            def h_tile(k, j):
                act.wait_ge(sq_used, 47 + k)
                act.wait_ge(h_ready, k + 1)
                act.activation(act_hi[:, k, :], h_t[:, k, :], ACT.Identity,
                               scale=cols[:, bass.ds(C_KVG + k, 1)]).then_inc(act_hi_done, 1)
                act.activation(sq1[:, j, :], h_t[:, k, :], ACT.Square).then_inc(sq_ready, 1)

            pairs(act, 0, 16, h_tile)
            act.dma_start(h_s.rearrange("k p t -> p k t"), h_t[:, :, :]).then_inc(h_stored, 16)
            deviation(3, var1, dev1)

            def k_block(m, j):
                high(N_KV + m + 2, j)
                store(N_KV + m, 48 + m, j, kv_s[m])

            pairs(act, 0, 12, k_block)

            def v_block(m, j):
                high(N_KV + 14 + m, j)
                value_out(m + 7, 59 + m, 1 - j, T, kv_s[m + 11])

            high(N_KV + 14, 0)
            high(N_KV + 15, 1)
            value_out(8, 60, 0, T, kv_s[12])
            pairs(act, 2, 12, v_block)
            value_out(19, 71, 1, T, kv_s[23])

            act.dma_start(fq[0:HEADS, 0, 0:1], bfg_d).then_inc(bfg_loaded, 16)
            high(N_FG + 2, 0)

            def again(k, j):
                act.activation(act_hi[:, k, :], h_t[:, k, :], ACT.Identity,
                               scale=cols[:, bass.ds(C_PRE + KD + k, 1)]).then_inc(act_hi_done, 1)

            act.wait_ge(gemm_done, N_INB)
            pairs(act, 0, 16, again)
            act.wait_ge(fg_ready, 1)
            act.activation(fgb[0:HEADS, :], fgb[0:HEADS, :], ACT.Exp, scale=-1.0).then_inc(fg_exp, 1)
            act.wait_ge(fg_exp, 1)
            act.activation(fgb[0:HEADS, :], fgb[0:HEADS, :], ACT.Ln, bias=c_one[0:HEADS]).then_inc(fg_ln, 1)

            act.wait_ge(fc_ready, 1)
            act.dma_start(fc_s, fgb[0:HEADS, :]).then_inc(fc_stored, 16)

            def q_block(m, j):
                high(N_INB + m + 2, (N_INB + j) % 2)
                store(N_INB + m, 72 + m, j, proj_b[m])

            pairs(act, 0, 16, q_block)

            def unit(t, j, memory):
                u = MEMH + t
                exps(u, s_b, [NM] * 4 if memory else [P, 2 * P, 3 * P, 4 * P], None)
                high(N_INB + 18 + t, (N_INB + j) % 2)
                act.wait_ge(out_taken, N_INB + 17 + t)
                wait(act, post_done, t - 1)
                act.activation(sz_b[:, j, :], z_b[:, j, :], ACT.Tanh, scale=0.5).then_inc(tanh_done, 1)
                if memory:
                    mem_pt(u, pt_b)
                    return
                act.wait_ge(turned, u + 1)
                act.wait_ge(att_done, u)
                for i, out in ((1, p6[:, 2 * P:T]), (3, pt[:, 0:T]), (2, pt[:, T:T + 3 * P]), (0, pt[:, T + 3 * P:2 * T])):
                    last = act.activation(pt_b[:, 0:i + 1, i * P:(i + 1) * P],
                                          out.rearrange("p (k q) -> p k q", q=P), ACT.Copy)
                    if i == 1:
                        last.then_inc(p6_copied, 1)
                last.then_inc(pt_ready, 1)

            unit(0, 0, False)
            unit(1, 1, False)
            pairs(act, 2, 12, lambda t, j: unit(t, j, False))
            for t in range(HEADS, UNITS):
                unit(t, t % 2, True)

            def cat_tile(k, j):
                act.wait_ge(post_done, k + 1)
                act.activation(act_hi[:, k, :], cat_t[:, k, :], ACT.Copy).then_inc(act_hi_done, 1)

            act.wait_ge(gemm_done, N_OUTB)
            pairs(act, 0, 16, cat_tile)
            out_b = out_block(N_OUTB, 64)
            act.wait_ge(act_lo_done, 96)
            pairs(act, 0, 14, out_b)
            out_b(14, 0, False)
            out_b(15, 1, False)
            deviation(4, var1, dev1)

        @block.vector
        def _(dve):
            st = Steps(dve, dve_seq)
            tt, ts, stt = nc.vector.tensor_tensor, nc.vector.tensor_scalar, nc.vector.scalar_tensor_tensor

            def total(q, slot, acc, sq, width=T):
                dve.wait_ge(sq_ready, q + 1)
                if isinstance(q, int) and q % 16 == 0:
                    ins = nc.vector.tensor_copy(acc[:, 0:width], sq[:, slot, 0:width])
                else:
                    dve.wait_ge(sq_used, q)
                    ins = tt(acc[:, 0:width], acc[:, 0:width], sq[:, slot, 0:width], ALU.add)
                ins.then_inc(sq_used, 1)

            def inverse_rms(e, r, var, dev, width=T):
                r, var, dev = r[:, 0:width], var[:, 0:width], dev[:, 0:width]
                dve.wait_ge(stat_done, e + 1)
                ts(var, p7[:, 0:width], 1.0 / D, EPS, ALU.mult, ALU.add).then_inc(var_ready, 1)
                dve.wait_ge(dev_ready, e + 1)
                st.link(nc.vector.reciprocal(r, dev))
                st.link(tt(dev, r, r, ALU.mult))
                st.link(tt(dev, dev, var, ALU.mult))
                st.link(ts(dev, dev, -0.5, 1.5, ALU.mult, ALU.add))
                tt(r, r, dev, ALU.mult).then_inc(r_ready, 1)
                dve.wait_ge(r_ready, e + 1)

            def low(c, dst, src, col, hi):
                dve.wait_ge(act_hi_done, c + 1)
                if col is None:
                    ins = tt(dst, src, hi.bitcast(F32), ALU.subtract)
                else:
                    ins = stt(dst, src, col, hi.bitcast(F32), ALU.mult, ALU.subtract)
                ins.then_inc(act_lo_done, 1)

            def take(n, slot, s, stage_slot, out=None, source=None, by=None):
                dve.wait_ge(gemm_done, n + 1)
                if s is not None:
                    wait(dve, stage_stored[stage_slot], half(s, stage_slot))
                out = stage[:, stage_slot, :] if out is None else out
                source = pgemm[:, slot, :] if source is None else source
                tt(out, source, rbc[:, :] if by is None else by, ALU.mult).then_inc(out_taken, 1)

            dve.wait_ge(cols_loaded, 16)
            ts(hbglu[:, :], cols[:, C_BGLU:C_BGLU + HEADS], 0.5, None, ALU.mult)

            for k in range(KD):
                src = xs[:, (k // 4) % 2, (k % 4) * NM:(k % 4 + 1) * NM]
                dve.wait_ge(act_hi_done, k + 1)
                c = C_MEMG + k
                stt(mact_lo[:, 0, k, :], src, cols[:, c:c + 1], mact_hi[:, 0, k, :].bitcast(F32),
                    ALU.mult, ALU.subtract)
                low(k, mact_lo[:, 1, k, :], src, cols[:, c + KD:c + KD + 1], mact_hi[:, 1, k, :])
                total(k, k % 2, acc0, sq0, NM)
            inverse_rms(0, rmem, var0, dev0, NM)

            def x_tile(k, slot):
                low(16 + k, act_lo[:, k, :], xs[:, slot, 0:T], cols[:, bass.ds(C_PRE + k, 1)], act_hi[:, k, :])
                total(16 + k, slot, acc0, sq0)

            for n in range(16):
                x_tile(n, n % 2)
                if n % 8 < MEMH:
                    take(n, n % 2, n, n % 2, stage[:, n % 2, 0:NM], pgemm[:, n % 2, 0:NM], rmem[:, :])
                else:
                    v = 4 * (n // 8) + n % 4
                    wait(dve, vturned, v - 1)
                    take(n, n % 2, None, None, vt0[:, n % 2, 0:NM], pgemm[:, n % 2, 0:NM], rmem[:, :])
            inverse_rms(1, rbc, var0, dev0)

            def u_block(m, j):
                def view(x):
                    return x.rearrange("p (c t) -> p c t", t=TC)
                take(N_INA + m, j, 16 + m, j, stage[:, j, :].rearrange("p (t c) -> p c t", t=TC),
                     view(pgemm[:, j, :]), view(rbc[:, :]))

            u_block(0, 0)
            u_block(1, 1)

            dve.wait_ge(lam_loaded, 16)
            la_re, la_im, step = (tB[:, i * GROUPS:(i + 1) * GROUPS] for i in range(3))
            tmp = [tA[:, i * GROUPS:(i + 1) * GROUPS] for i in range(12)]
            decay_i = decay[:, 0:GROUPS].bitcast(I32)

            def exp_parts(z, scale, em1, t):
                st.link(ts(z, z, -87.0, 88.0, ALU.max, ALU.min))
                st.link(ts(t, z, LOG2E, MAGIC, ALU.mult, ALU.add))
                st.link(ts(t, t, MAGIC, None, ALU.subtract))
                st.link(stt(z, t, -LN2_A, z, ALU.mult, ALU.add))
                st.link(stt(z, t, -LN2_B, z, ALU.mult, ALU.add))
                st.link(ts(decay_i, t, 127.0, None, ALU.add))
                st.link(ts(decay_i, decay_i, 23, None, ALU.logical_shift_left))
                st.link(nc.vector.tensor_copy(scale, decay[:, 0:GROUPS]))
                st.link(ts(em1, z, 1.0 / 5040, None, ALU.mult))
                for c in (1.0 / 720, 1.0 / 120, 1.0 / 24, 1.0 / 6, 0.5, 1.0):
                    st.link(stt(em1, em1, c, z, ALU.add, ALU.mult))

            def reduce_angle(x, t):
                st.link(ts(t, x, INV_2PI, MAGIC, ALU.mult, ALU.add))
                st.link(ts(t, t, MAGIC, None, ALU.subtract))
                for part in (PI2_A, PI2_B, PI2_C):
                    st.link(stt(x, t, -part, x, ALU.mult, ALU.add))
                st.link(ts(x, x, -PI, PI, ALU.max, ALU.min))

            scale, em1, t0, dt, mag, mag_m1, omega, ar, ai, ar_m1, t1, t2 = tmp
            exp_parts(step, scale, em1, t0)
            st.link(stt(dt, em1, 1.0, scale, ALU.add, ALU.mult))
            st.link(tt(t1, la_re, dt, ALU.mult))
            exp_parts(t1, scale, em1, t0)
            st.link(stt(mag, em1, 1.0, scale, ALU.add, ALU.mult))
            st.link(tt(em1, em1, scale, ALU.mult))
            st.link(stt(mag_m1, scale, -1.0, em1, ALU.add, ALU.add))
            st.link(tt(omega, la_im, dt, ALU.mult))
            reduce_angle(omega, t0)
            st.link(nc.vector.tensor_copy(bco[:, 0, :], omega))
            nc.vector.tensor_copy(bco[:, 1, :], omega).then_inc(sin_asked, 1)
            dve.wait_ge(sin_asked, 1)
            pairs(dve, 2, 4, u_block)
            st.link(ts(omega8[:, :], omega, float(TC), None, ALU.mult))
            reduce_angle(omega8[:, :], t0)
            st.link(ts(omega8[:, :], omega8[:, :], INV_2PI, None, ALU.mult))
            st.link(tt(mag8[:, :], mag, mag, ALU.mult))
            st.link(tt(mag8[:, :], mag8[:, :], mag8[:, :], ALU.mult))
            st.link(tt(mag8[:, :], mag8[:, :], mag8[:, :], ALU.mult))
            dve.wait_ge(sin_done, 2)
            st.link(tt(t1, bco[:, 1, :], bco[:, 1, :], ALU.mult))
            st.link(ts(t1, t1, -2.0, None, ALU.mult))
            st.link(tt(t1, t1, mag, ALU.mult))
            st.link(tt(ar_m1, t1, mag_m1, ALU.add))
            st.link(ts(ar, ar_m1, 1.0, None, ALU.add))
            st.link(tt(ai, mag, bco[:, 0, :], ALU.mult))
            st.link(tt(t0, la_re, la_re, ALU.mult))
            st.link(tt(t1, la_im, la_im, ALU.mult))
            st.link(tt(t0, t0, t1, ALU.add))
            st.link(nc.vector.reciprocal(dt, t0))
            st.link(tt(t0, ar_m1, la_re, ALU.mult))
            st.link(tt(t1, ai, la_im, ALU.mult))
            st.link(tt(t0, t0, t1, ALU.add))
            st.link(tt(bco[:, 0, :], t0, dt, ALU.mult))
            st.link(tt(t0, ai, la_re, ALU.mult))
            st.link(tt(t1, ar_m1, la_im, ALU.mult))
            st.link(tt(t0, t0, t1, ALU.subtract))
            st.link(tt(bco[:, 1, :], t0, dt, ALU.mult))
            st.link(ts(bco[:, 2, :], bco[:, 0, :], c_sgn, None, ALU.mult))
            st.link(ts(bco[:, 3, :], bco[:, 1, :], c_sgn, None, ALU.mult))
            st.link(nc.vector.memset(up_re[:, :, 0], 1.0))
            st.link(nc.vector.memset(up_im[:, :, 0], 0.0))
            st.link(nc.vector.tensor_copy(up_re[:, :, 1], ar))
            st.link(nc.vector.tensor_copy(up_im[:, :, 1], ai))
            for have in (1, 2, 4):
                lo_r, lo_i = up_re[:, :, 1:have + 1], up_im[:, :, 1:have + 1]
                by_r, by_i = (x[:, :, have:have + 1].broadcast_to([P, GROUPS, have]) for x in (up_re, up_im))
                new_r, new_i = (x[:, :, have + 1:2 * have + 1] for x in (up_re, up_im))
                wa = tA[:, 0:GROUPS * have].rearrange("p (g k) -> p g k", k=have)
                wb = tA[:, GROUPS * 4:GROUPS * (4 + have)].rearrange("p (g k) -> p g k", k=have)
                st.link(tt(wa, lo_r, by_r, ALU.mult))
                st.link(tt(wb, lo_i, by_i, ALU.mult))
                st.link(tt(new_r, wa, wb, ALU.subtract))
                st.link(tt(wa, lo_r, by_i, ALU.mult))
                st.link(tt(wb, lo_i, by_r, ALU.mult))
                st.link(tt(new_i, wa, wb, ALU.add))
            for k in range(TC):
                nc.vector.tensor_copy(dn_re[:, :, k], up_re[:, :, TC - 1 - k])
                st.mark(nc.vector.tensor_copy(dn_im[:, :, k], up_im[:, :, TC - 1 - k]))
            st.sync()
            pairs(dve, 4, 6, u_block)

            def wide(x, n):
                return x.rearrange("p (g h) -> p g h", g=GB).unsqueeze(2).broadcast_to([P, GB, n, 16])

            def params(b, j, first=False):
                dve.wait_ge(bc_loaded, b * 16 + 16)
                wait(dve, lags_done, b)
                grp = bass.ds(b * GB, GB)

                def co(i):
                    return bco[:, i, grp].unsqueeze(2).broadcast_to([P, GB, 16])

                def gh(x):
                    return x.rearrange("p (g h) -> p g h", g=GB)
                b_st, b_sw, c_st, c_sw = (gh(bcp[:, i, :]) for i in range(4))
                w0, w1, w2, w3 = (gh(bbar[:, i, :]) for i in range(4))
                st.mark(tt(w0, b_st, co(0), ALU.mult))
                st.mark(tt(w1, b_sw, co(3), ALU.mult))
                st.mark(tt(w2, b_sw, co(2), ALU.mult))
                st.link(tt(w3, b_st, co(1), ALU.mult))
                st.mark(tt(w0, w0, w1, ALU.add))
                st.link(tt(w3, w2, w3, ALU.subtract))
                st.mark(nc.vector.tensor_copy(
                    bdiag[:, :].rearrange("p (g c) -> p g c", g=GB)[:, :, 0:16], w0))
                st.mark(ts(bbar[:, 1, :], bcp[:, 2, :], c_nsgn, None, ALU.mult))
                st.link(ts(bbar[:, 2, :], bcp[:, 3, :], -1.0, None, ALU.mult))
                if not first:
                    dve.wait_ge(trig_done, b)
                x4 = tA[:, 0:GB * P].rearrange("p (g h t) -> p g h t", g=GB, h=16)

                def tall(x):
                    return gh(x).unsqueeze(3).broadcast_to([P, GB, 16, TC])

                def down(x):
                    return x[:, grp, :].unsqueeze(2).broadcast_to([P, GB, 16, TC])
                st.mark(tt(gst[:, :, :, :], tall(bbar[:, 0, :]), down(dn_re), ALU.mult))
                st.link(tt(x4, tall(bbar[:, 3, :]), down(dn_im), ALU.mult))
                st.link(tt(gst[:, :, :, :], gst[:, :, :, :], x4, ALU.add))
                wait(dve, ssm_y_done, b - 1)

                def up(x, first, n):
                    return x[:, grp, first:first + n].unsqueeze(3).broadcast_to([P, GB, n, 16])
                n9 = TC + 1
                y4 = tA[:, :].rearrange("p (g l h) -> p g l h", g=GB, l=n9)
                st.mark(tt(hc[:, j, :, :, :], wide(bbar[:, 1, :], n9), up(up_re, 0, n9), ALU.mult))
                st.link(tt(y4, wide(bbar[:, 2, :], n9), up(up_im, 0, n9), ALU.mult))
                st.link(tt(hc[:, j, :, :, :], hc[:, j, :, :, :], y4, ALU.add))
                z4 = tA[:, 0:GB * P].rearrange("p (g l h) -> p g l h", g=GB, l=TC)
                st.mark(tt(hrot[:, j, :, :, :], wide(bbar[:, 2, :], TC), up(up_re, 1, TC), ALU.mult))
                st.link(tt(z4, wide(bbar[:, 1, :], TC), up(up_im, 1, TC), ALU.mult))
                tt(hrot[:, j, :, :, :], hrot[:, j, :, :, :], z4, ALU.subtract).then_inc(params_ready, 1)
                dve.wait_ge(params_ready, b + 1)

            def phases(b, j):
                grp = bass.ds(b * GB, GB)

                def gc(x):
                    return x.rearrange("p (g c) -> p g c", g=GB)
                turns, whole = tB[:, :], tA[:, 0:T]
                st.link(tt(gc(turns), omega8[:, grp].unsqueeze(2).broadcast_to([P, GB, NC]),
                           cidx[:, :].unsqueeze(1).broadcast_to([P, GB, NC]), ALU.mult))
                st.link(ts(whole, turns, MAGIC, None, ALU.add))
                st.link(stt(turns, whole, MAGIC, turns, ALU.subtract, ALU.subtract))
                st.mark(nc.vector.tensor_copy(gc(decay[:, :]), mag8[:, grp].unsqueeze(2).broadcast_to([P, GB, NC])))
                st.sync()
                st.mark(nc.vector.memset(gc(decay[:, :])[:, :, 0:1], 0.0))
                stt(whole, turns, -1.0, turns, ALU.mult, ALU.max).then_inc(phase_ready, 1)

            def rotate_scan(b, j):
                dve.wait_ge(states_done, b + 1)
                st.mark(tt(tB[:, :], ps[:, 0, :], cos_t[:, :], ALU.mult))
                st.link(tt(tA[:, 0:T], ps[:, 1, :], sin_t[:, :], ALU.mult))
                st.link(tt(tA[:, 0:T], tA[:, 0:T], tB[:, :], ALU.add))
                st.link(nc.vector.tensor_tensor_scan(tB[:, :], decay[:, :], tA[:, 0:T], 0.0, ALU.mult, ALU.add))
                wait(dve, ssm_y_done, b)

                def part(x, first):
                    return x.rearrange("p (g c) -> p g c", g=GB)[:, :, first:first + NC - 1]
                st.mark(tt(x1[:, :, 1:NC], part(tB[:, :], 0), part(cos_t[:, :], 0), ALU.mult))
                tt(x2[:, :, 1:NC], part(tB[:, :], 0), part(sin_t[:, :], 0), ALU.mult).then_inc(rot_done, 1)

            params(0, 0, first=True)
            pairs(dve, 6, 12, u_block)

            def batch(b, j):
                if not isinstance(b, int) or b > 0:
                    rotate_scan(b - 1, 1 - j)
                    dve.wait_ge(rot_done, b)
                phases(b, j)
                if not isinstance(b, int) or b < NB - 1:
                    params(b + 1, 1 - j)
                take(N_INA + 12 + b, j, 28 + b, j)

            batch(0, 0)
            batch(1, 1)
            st.loop(2, 10, 27, batch)
            batch(10, 0)
            batch(11, 1)
            rotate_scan(11, 1)
            take(N_INA + 24, 0, 40, 0)
            take(N_INA + 25, 1, 41, 1)

            def gelu_block(i, j):
                for slot in (0, 1):
                    m = i * 2 + slot
                    dve.wait_ge(yu_loaded[slot], i * 144 + 144)
                    wait(dve, yg_done, i * 2)
                    stt(yv[:, slot, :].rearrange("p (c t) -> p t c", t=TC),
                        um[:, slot, :].rearrange("p (t c) -> p t c", t=TC), cols[:, bass.ds(C_DSKIP + m, 1)],
                        ym[:, slot, :].rearrange("p (t c) -> p t c", t=TC), ALU.mult, ALU.add).then_inc(yv_ready, 1)
                for slot in (0, 1):
                    dve.wait_ge(ysq_done, i * 2 + slot + 1)
                    st.mark(ts(yq[:, slot, :], yq[:, slot, :], 0.044715, 1.0, ALU.mult, ALU.add))
                st.sync()
                for slot in (0, 1):
                    tt(yq[:, slot, :], yq[:, slot, :], yv[:, slot, :], ALU.mult).then_inc(yin_ready, 1)
                for slot in (0, 1):
                    dve.wait_ge(yth_done, i * 2 + slot + 1)
                    stt(yv[:, slot, :], yth[:, slot, :], 1.0, yv[:, slot, :], ALU.add, ALU.mult).then_inc(yg_ready, 1)
                for slot in (0, 1):
                    m = i * 2 + slot
                    dve.wait_ge(yghi_done, m + 1)
                    stt(yg_lo[:, m, :], yv[:, slot, :], 0.5, yg_hi[:, m, :].bitcast(F32), ALU.mult,
                        ALU.subtract).then_inc(yg_done, 1)
                take(N_INA + 26 + i, j, 42 + i, j)

            dve.wait_ge(ssm_y_done, NB)
            gelu_block(0, 0)
            gelu_block(1, 1)
            st.loop(2, 6, 2, gelu_block)

            def softmax_max(u, s, widths, source):
                dve.wait_ge(scores_done, u + 1)
                wait(dve, turned, u)
                for i, w in enumerate(widths):
                    source(i, w)
                st.sync()
                for i, w in enumerate(widths):
                    last = nc.vector.tensor_reduce(nmax[:, i:i + 1], s[:, i, 0:w], AX.X, ALU.max, negate=True)
                last.then_inc(max_ready, 1)

            def softmax_scale(u, s, widths):
                dve.wait_ge(exp_done, u + 1)
                st.link(nc.vector.reciprocal(rsum[:, :], rsum[:, :]))
                for i, w in enumerate(widths):
                    last = ts(s[:, i, 0:w], s[:, i, 0:w], rsum[:, i:i + 1], None, ALU.mult)
                last.then_inc(probs_ready, 1)

            def scores_to(s, scale):
                def source(i, w):
                    st.mark(ts(s[:, i, 0:w], ps[:, i // 2, (i % 2) * NM:(i % 2) * NM + w], scale, None, ALU.mult))
                return source

            def gate_block(g, j):
                n, c = N_GLU + g, joined_main(g)
                if isinstance(g, int) and 1 <= g <= MEMH:
                    softmax_max(g - 1, s_a, [NM] * 4, scores_to(s_a, SCALE))
                    softmax_scale(g - 1, s_a, [NM] * 4)
                dve.wait_ge(act_lo_done, 32 + c)
                dve.wait_ge(tz_done, c + 1)
                dve.wait_ge(out_taken, n + 1)
                st.mark(tt(y2_a[:, :], yg_hi[:, g, :].bitcast(F32), yg_lo[:, g, :].bitcast(F32), ALU.add))
                st.link(stt(sz_a[:, :], tz_a[:, :], 1.0, z_a[:, j, :], ALU.add, ALU.mult))
                st.link(stt(y2_a[:, :], tg_a[:, :], 1.0, y2_a[:, :], ALU.add, ALU.mult))
                tt(y2_a[:, :], y2_a[:, :], sz_a[:, :], ALU.mult).then_inc(main_ready, 1)
                dve.wait_ge(main_ready, c + 1)
                low_joined(32 + c, act_lo[:, g, :], 0.25, act_hi[:, g, :])
                if isinstance(g, int) and 2 <= g <= MEMH + 1:
                    u = g - 2
                    dve.wait_ge(tz_done, c + 2)
                    st.link(stt(sz_a[:, :], tz_a[:, :], 1.0, zm_a[:, :], ALU.add, ALU.mult))
                    dve.wait_ge(att_done, u + 1)
                    dve.wait_ge(act_lo_done, 33 + c)
                    tt(y2_a[:, :], p7[:, :], sz_a[:, :], ALU.mult).then_inc(main_ready, 1)
                    dve.wait_ge(main_ready, c + 2)
                    low_joined(33 + c, act_lo[:, HEADS + u, :], 0.5, act_hi[:, HEADS + u, :])

            def low_joined(c, dst, scale, hi):
                dve.wait_ge(act_hi_done, c + 1)
                stt(dst, y2_a[:, :], scale, hi.bitcast(F32), ALU.mult, ALU.subtract).then_inc(act_lo_done, 1)

            for g in range(6):
                gate_block(g, g % 2)
            st.loop(6, 12, 3, gate_block)

            total(32, 0, acc1, sq1)
            total(33, 1, acc1, sq1)
            pairs(dve, 2, 16, lambda m, j: total(32 + m, j, acc1, sq1))
            inverse_rms(2, rbc, var1, dev1)
            dve.wait_ge(x_loaded, 16)

            def residual(k, layer, c):
                col = cols[:, bass.ds(C_POST + layer * KD + k, 1)]
                st.link(stt(o_t[:, k, :], o_t[:, k, :], col, rbc[:, :], ALU.mult, ALU.mult))
                tt(h_t[:, k, :], h_t[:, k, :], o_t[:, k, :], ALU.add).then_inc(h_ready, 1)

            def h_low(k):
                low(48 + k, act_lo[:, k, :], h_t[:, k, :], cols[:, bass.ds(C_KVG + k, 1)], act_hi[:, k, :])

            def h_tile(k, j):
                residual(k, 0, k)
                h_low(k - 1)

            residual(0, 0, 0)
            h_tile(1, 1)
            st.loop(2, 16, 1, h_tile)
            h_low(15)
            inverse_rms(3, rbc, var1, dev1)
            pairs(dve, 0, 12, lambda m, j: take(N_KV + m, j, 48 + m, j))

            def v_block(m, j):
                wait(dve, vturned, m + 7)
                take(N_KV + 12 + m, j, None, None, vt1[:, j, :])

            pairs(dve, 0, 12, v_block)

            dve.wait_ge(gemm_done, N_FG + 1)
            dve.wait_ge(bfg_loaded, 16)
            fa, fb = fga[0:HEADS, :], fgb[0:HEADS, :]
            tt(fa, pgemm[0:HEADS, N_FG % 2, :], rbc[0:HEADS, :], ALU.mult).then_inc(out_taken, 1)
            dve.wait_ge(out_taken, N_FG + 1)

            def again(k, j):
                low(64 + k, act_lo[:, k, :], h_t[:, k, :], cols[:, bass.ds(C_PRE + KD + k, 1)], act_hi[:, k, :])

            pairs(dve, 0, 16, again)

            st.link(ts(fa, fa, fq[0:HEADS, 0, 0:1], None, ALU.add))
            stt(fb, fa, -1.0, fa, ALU.mult, ALU.max).then_inc(fg_ready, 1)
            dve.wait_ge(fg_ready, 1)
            st.link(ts(fa, fa, 0.0, None, ALU.min))
            dve.wait_ge(fg_ln, 1)
            st.link(tt(fa, fa, fb, ALU.subtract))
            st.link(nc.vector.memset(fb, 1.0))
            st.link(nc.vector.tensor_tensor_scan(fb, fb, fa, 0.0, ALU.mult, ALU.add))
            ts(fb, fb, -1.0, None, ALU.mult).then_inc(fc_ready, 1)

            def q_block(m, j):
                n, slot = N_INB + m, (N_INB + j) % 2
                dve.wait_ge(gemm_done, n + 1)
                wait(dve, stage_stored[j], half(72 + m, j))
                stt(stage[:, j, :], pgemm[:, slot, :], SCALE, rbc[:, :], ALU.mult, ALU.mult).then_inc(out_taken, 1)

            q_block(0, 0)
            dve.wait_ge(fq_turned, 1)
            ts(fq[:, :, :], pt[:, 0:4 * HEADS].rearrange("p (i h) -> p i h", i=4), -1.0, None,
               ALU.mult).then_inc(fq_ready, 1)
            q_block(1, 1)
            pairs(dve, 2, 16, q_block)
            dve.wait_ge(fq_ready, 1)
            dve.wait_ge(h_stored, 16)

            fox_widths = [P, 2 * P, 3 * P, 4 * P]
            fox_out = [ps[:, 0, 0:P], p6[:, 0:2 * P], ps[:, 0, P:4 * P], ps[:, 1, :]]

            def fox_softmax(t, j):
                def source(i, w):
                    st.link(stt(s_b[:, i, 0:w], fox_out[i], fq[:, i, bass.ds(t, 1)], bias_b[:, j, 0:w],
                                ALU.add, ALU.add))
                    diag = s_b[:, i, w - P:w]
                    st.mark(tt(diag, diag, mask[:, :], ALU.add))
                softmax_max(MEMH + t, s_b, fox_widths, source)
                softmax_scale(MEMH + t, s_b, fox_widths)

            def post(t, j):
                dve.wait_ge(att_done, MEMH + t + 1)
                stt(cat_t[:, t, :], p7[:, :], 0.5, sz_b[:, j, :], ALU.mult, ALU.mult).then_inc(post_done, 1)

            def z_tile(t, j):
                take(N_INB + 16 + t, (N_INB + j) % 2, None, None, z_b[:, j, :])
                if not isinstance(t, int) or t > 0:
                    post(t - 1, 1 - j)
                dve.wait_ge(tanh_done, t + 1)
                st.link(stt(sz_b[:, j, :], sz_b[:, j, :], 1.0, z_b[:, j, :], ALU.add, ALU.mult))

            def fox_unit(t, j):
                dve.wait_ge(qk_loaded[j], half(t, j) * 3 + 48)
                fox_softmax(t, j)
                z_tile(t, j)

            fox_unit(0, 0)
            fox_unit(1, 1)
            st.loop(2, 12, 10, fox_unit)
            for t in range(HEADS, UNITS):
                softmax_max(MEMH + t, s_b, [NM] * 4, scores_to(s_b, 1.0))
                softmax_scale(MEMH + t, s_b, [NM] * 4)
                z_tile(t, t % 2)
            post(15, 1)

            def cat_tile(k, j):
                low(80 + k, act_lo[:, k, :], cat_t[:, k, :], None, act_hi[:, k, :])

            dve.wait_ge(post_done, UNITS)
            pairs(dve, 0, 16, cat_tile)
            total(64, 0, acc1, sq1)
            total(65, 1, acc1, sq1)
            pairs(dve, 2, 16, lambda m, j: total(64 + m, j, acc1, sq1))
            inverse_rms(4, rbc, var1, dev1)
            dve.wait_ge(h_loaded, 16)
            st.loop(0, 16, 1, lambda k, j: residual(k, 1, k))


def kernel(x, mem, pre_norm_g, post_norm_g, w_in_a, lam_re, lam_im, log_step, b_re, b_im, c_re, c_im, d_skip,
           w_glu, b_glu, kv_norm_g, w_kv, w_fgate, b_fgate, w_in_b, mem_norm_g, w_mem_kv, w_out):
    import numpy as np
    import concourse.bacc as bacc
    from concourse.bass_utils import run_bass_kernel_spmd

    def tiles(a):
        return a.T.reshape(-1, P, a.shape[0])

    def blocks(w):
        k, m = w.shape
        return w.reshape(k // P, P, m // P, P).transpose(2, 1, 0, 3).reshape(m // P, P, -1)

    def columns(g):
        return g.reshape(-1, P).T

    def twice(a):
        return np.concatenate([a.T, a.T])

    def batches(top, bottom):
        a = np.concatenate([top, bottom], axis=1).reshape(NB, GB, P, 16)
        return a.transpose(0, 2, 1, 3).reshape(NB, P, P)

    cols = np.concatenate([columns(g) for g in (pre_norm_g, post_norm_g, kv_norm_g, mem_norm_g, b_glu, d_skip)], axis=1)
    steps = np.broadcast_to(log_step[0][None, :], (P, GROUPS))
    c_r, c_i = c_re[0].transpose(0, 2, 1), c_im[0].transpose(0, 2, 1)
    fg = np.zeros((D, P), w_fgate.dtype)
    fg[:, :HEADS] = w_fgate
    b_blocks = blocks(w_in_b[0])
    ins = {
        "x_t": tiles(x[0]), "mem_t": tiles(mem[0]), "cols_d": cols, "bfg_d": b_fgate.reshape(HEADS, 1),
        "lam_d": np.concatenate([twice(lam_re[0]), twice(lam_im[0]), steps], axis=1),
        "bc_d": np.stack([batches(b_re[0], b_im[0]), batches(b_im[0], b_re[0]), batches(c_r, c_i),
                          batches(c_i, c_r)], axis=2),
        "w_mem": np.concatenate([blocks(w_mem_kv[0]), blocks(w_mem_kv[1])]), "w_in_a": blocks(w_in_a[0]),
        "w_glu": blocks(w_glu[0]), "w_out": np.stack([blocks(w_out[0]), blocks(w_out[1])]), "w_kv": blocks(w_kv),
        "w_fg": blocks(fg),
        "w_in_b": np.concatenate([b_blocks[0:12], b_blocks[24:28], b_blocks[12:24], b_blocks[28:32]]),
    }
    nc = bacc.Bacc("TRN2", target_bir_lowering=False, num_devices=1)
    arrays = {name: np.ascontiguousarray(a) for name, a in ins.items()}
    args = [nc.dram_tensor(name, a.shape, mybir.dt.from_np(a.dtype), kind="ExternalInput").ap()
            for name, a in arrays.items()]
    out = nc.dram_tensor("out_t", (KD, P, T), F32, kind="ExternalOutput").ap()
    trunk(nc, *args, out)
    r = run_bass_kernel_spmd(nc, [arrays], core_ids=[0])
    return r.results[0]["out_t"].reshape(D, T).T[None]
```

```python
from contextlib import ExitStack

import concourse.bass as bass
from concourse import mybir

P = 128
T = 512
D = 2048
KD = D // P
NM = 256
HEADS = 12
MEMH = 4
UNITS = HEADS + MEMH
GROUPS = 96
GB = 8
NB = GROUPS // GB
TC = 8
NC = T // TC
IN_T = 32
LAG = 6
TAIL = 10
EPS = 1e-6
SCALE = P ** -0.5

N_MEM, N_INA, N_GLU, N_OUTA, N_KV, N_FG, N_INB, N_OUTB, N_BLOCKS = 0, 16, 48, 60, 76, 100, 101, 133, 149

C_PRE, C_POST, C_KVG, C_MEMG, C_BGLU, C_DSKIP, N_COLS = 0, 32, 64, 80, 112, 124, 136

F32 = mybir.dt.float32
F32R = mybir.dt.float32r
I32 = mybir.dt.int32
ALU = mybir.AluOpType
ACT = mybir.ActivationFunctionType
AX = mybir.AxisListType

MAGIC = 12582912.0
INV_2PI = 0.15915494309189535
PI2_A = 6.28125
PI2_B = 0.001934051513671875
PI2_C = 1.255665914356996e-06
PI = 3.1415925
TWO_PI = 6.283185
HALF_PI = 1.5707963
LOG2E = 1.4426950408889634
LN2_A = 0.693359375
LN2_B = -2.12194440e-4
GELU_C = 0.7978845608028654
MASKED = -3.0e38


def trunk(nc, x_t, mem_t, cols_d, bfg_d, lam_d, bc_d, w_mem, w_in_a, w_glu, w_out, w_kv, w_fg, w_in_b, out_t):
    with ExitStack() as ctx:
        def dram(name, shape):
            return nc.dram_tensor(name, shape, F32, kind="Internal").ap()

        def sem(name):
            return ctx.enter_context(nc.semaphore(name))

        def sb(name, shape, dt=F32, stack=ctx):
            return stack.enter_context(nc.sbuf_tensor(name, shape, dt))

        proj_a = dram("proj_a", (IN_T, P, T))
        proj_b = dram("proj_b", (UNITS, P, T))
        y_s = dram("y_s", (NB, GB, P, NC))
        kv_s = dram("kv_s", (2 * HEADS, P, T))
        mem_s = dram("mem_s", (4 * MEMH, P, NM))
        lag_s = dram("lag_s", (2, P, (2 * TC - 1) * 16))
        fc_s = dram("fc_s", (HEADS, T))
        h_s = dram("h_s", (KD, P, T))

        raw = [sb(f"raw{i}", [P, KD * P]) for i in range(2)]
        w_hi = [sb(f"w_hi{i}", [P, KD, P], F32R) for i in range(2)]
        w_lo = [sb(f"w_lo{i}", [P, KD, P], F32R) for i in range(2)]
        act_hi = sb("act_hi", [P, KD, T], F32R)
        act_lo = sb("act_lo", [P, KD, T], F32R)
        stage = sb("stage", [P, 2, T])
        rbc = sb("rbc", [P, T])
        ident = sb("ident", [P, P])
        ones = sb("ones", [P, P])
        cols = sb("cols", [P, N_COLS])
        hbglu = sb("hbglu", [P, HEADS])
        consts = sb("consts", [P, 4])
        c_half_pi, c_sgn, c_nsgn, c_one = (consts[:, i:i + 1] for i in range(4))

        mask = sb("mask", [P, P])
        var, dev, rcol = (sb(name, [P, 4]) for name in ("var", "dev", "rcol"))
        nmax = sb("nmax", [P, 4])
        rsum = sb("rsum", [P, 4])

        def overlay(specs):
            with ExitStack() as s:
                return [sb(name, shape, dt, s) for name, shape, dt in specs]

        mact_hi, mact_lo, acc0, sq0, diag0, xs, vt0, rmem = overlay([
            ("mact_hi", [P, 2, KD, NM], F32R), ("mact_lo", [P, 2, KD, NM], F32R),
            ("acc0", [P, T], F32), ("sq0", [P, 2, T], F32), ("diag0", [P, T], F32),
            ("xs", [P, 2, T], F32), ("vt0", [P, 2, T], F32), ("rmem", [P, NM], F32)])
        (_, _, mem_raw) = overlay([("under_hi", [P, 2, KD, NM], F32), ("under_lo", [P, KD, NM], F32),
                                   ("mem_raw", [P, KD, NM], F32)])
        (gst, hc, hrot, g1, g2, toep, ublk, x1, x2, cos_t, sin_t, decay, tA, tB, up_re, up_im,
         dn_re, dn_im, bcp, bbar, bdiag, lagpad, ystage, omega8, mag8, cidx, bco) = overlay([
            ("gst", [P, GB, 16, TC], F32), ("hc", [P, 2, GB, TC + 1, 16], F32),
            ("hrot", [P, 2, GB, TC, 16], F32),
            ("g1", [P, GB, P], F32), ("g2", [P, GB, P], F32), ("toep", [P, 2, GB, P], F32),
            ("ublk", [P, 2, GB, NC], F32), ("x1", [P, GB, NC], F32), ("x2", [P, GB, NC], F32),
            ("cos_t", [P, T], F32), ("sin_t", [P, T], F32), ("decay", [P, T], F32),
            ("tA", [P, GB * 16 * (TC + 1)], F32), ("tB", [P, T], F32),
            ("up_re", [P, GROUPS, TC + 1], F32), ("up_im", [P, GROUPS, TC + 1], F32),
            ("dn_re", [P, GROUPS, TC], F32), ("dn_im", [P, GROUPS, TC], F32),
            ("bcp", [P, 4, P], F32), ("bbar", [P, 4, P], F32), ("bdiag", [P, GB * (P + 16)], F32),
            ("lagpad", [P, 2 * TC - 1, 16], F32), ("ystage", [P, T], F32),
            ("omega8", [P, GROUPS], F32), ("mag8", [P, GROUPS], F32),
            ("cidx", [P, NC], F32), ("bco", [P, 4, GROUPS], F32)])
        yg_hi, yg_lo, ym, um, yv, yq, yth = overlay([
            ("yg_hi", [P, HEADS, T], F32R), ("yg_lo", [P, HEADS, T], F32R),
            ("ym", [P, 2, T], F32), ("um", [P, 2, T], F32), ("yv", [P, 2, T], F32), ("yq", [P, 2, T], F32),
            ("yth", [P, 2, T], F32)])
        (_, q_a, k_a, v_a, s_a, p_a, z_a, zm_a, tz_a, tg_a, y2_a, sz_a) = overlay([
            ("under_yg", [P, 2, HEADS, T], F32),
            ("q_a", [P, MEMH, T], F32), ("k_a", [P, MEMH, NM], F32), ("v_a", [P, MEMH, NM], F32),
            ("s_a", [P, 4, NM], F32), ("p_a", [P, 2, T], F32), ("z_a", [P, 2, T], F32), ("zm_a", [P, T], F32),
            ("tz_a", [P, T], F32), ("tg_a", [P, T], F32), ("y2_a", [P, T], F32), ("sz_a", [P, T], F32)])
        o_t, h_t, vt1, acc1, sq1, diag1, fga, fgb, fq = overlay([
            ("o_t", [P, KD, T], F32), ("h_t", [P, KD, T], F32), ("vt1", [P, 2, T], F32),
            ("acc1", [P, T], F32), ("sq1", [P, 2, T], F32), ("diag1", [P, T], F32),
            ("fga", [P, T], F32), ("fgb", [P, T], F32), ("fq", [P, 4, HEADS], F32)])
        (s_b, pt_b, q_b, k_b, v_b, bias_b, cat_t, z_b, sz_b, _) = overlay([
            ("s_b", [P, 4, T], F32), ("pt_b", [P, 4, T], F32), ("q_b", [P, 2, T], F32), ("k_b", [P, 2, T], F32),
            ("v_b", [P, 2, T], F32), ("bias_b", [P, 2, T], F32), ("cat_t", [P, KD, T], F32),
            ("z_b", [P, 2, T], F32), ("sz_b", [P, 2, T], F32), ("tail", [P, 2, T], F32)])
        pgemm = ctx.enter_context(nc.psum_tensor("pgemm", [P, 2, T], F32))
        pt = ctx.enter_context(nc.psum_tensor("pt", [P, 2 * T], F32))
        ps = ctx.enter_context(nc.psum_tensor("ps", [P, 2, T], F32))
        p6 = ctx.enter_context(nc.psum_tensor("p6", [P, T], F32))
        p7 = ctx.enter_context(nc.psum_tensor("p7", [P, T], F32))

        raw_loaded = [sem("raw_loaded0"), sem("raw_loaded1")]
        hi_done, lo_done, gemm_done, out_taken = sem("hi_done"), sem("lo_done"), sem("gemm_done"), sem("out_taken")
        cols_loaded, consts_ready = sem("cols_loaded"), sem("consts_ready")
        xs_loaded = [sem("xs_loaded0"), sem("xs_loaded1")]
        act_hi_done, act_lo_done = sem("act_hi_done"), sem("act_lo_done")
        sq_ready, sq_used = sem("sq_ready"), sem("sq_used")
        stat_done, var_ready, dev_ready, r_ready = sem("stat_done"), sem("var_ready"), sem("dev_ready"), sem("r_ready")
        diag_ready, spread_done = sem("diag_ready"), sem("spread_done")
        mem_loaded = [sem(f"mem_loaded{g}") for g in range(4)]
        mem_hi_done, mem_lo_done = sem("mem_hi_done"), sem("mem_lo_done")
        stage_stored = [sem("stage_stored0"), sem("stage_stored1")]
        vturned, vstaged = sem("vturned"), sem("vstaged")
        lam_loaded, sin_asked, sin_done = sem("lam_loaded"), sem("sin_asked"), sem("sin_done")
        region_clear = sem("region_clear")
        bc_loaded, toep_loaded = sem("bc_loaded"), [sem("toep_loaded0"), sem("toep_loaded1")]
        ublk_loaded = [sem("ublk_loaded0"), sem("ublk_loaded1")]
        params_ready, lags_done, g_ready, lag_stored = sem("params_ready"), sem("lags_done"), sem("g_ready"), sem("lag_stored")
        phase_ready, trig_done, states_done, rot_done = sem("phase_ready"), sem("trig_done"), sem("states_done"), sem("rot_done")
        ssm_y_done, y_taken, y_stored = sem("ssm_y_done"), sem("y_taken"), sem("y_stored")
        yu_loaded = [sem("yu_loaded0"), sem("yu_loaded1")]
        yv_ready, ysq_done, yin_ready, yth_done, yg_ready, yghi_done, yg_done = (
            sem(s) for s in ("yv_ready", "ysq_done", "yin_ready", "yth_done", "yg_ready", "yghi_done", "yg_done"))
        z_loaded = [sem("z_loaded0"), sem("z_loaded1")]
        zm_loaded, mq_loaded = sem("zm_loaded"), [sem(f"mq_loaded{u}") for u in range(MEMH)]
        tz_done, main_ready = sem("tz_done"), sem("main_ready")
        qk_loaded = [sem("qk_loaded0"), sem("qk_loaded1")]
        v_loaded = [sem("v_loaded0"), sem("v_loaded1")]
        scores_done, max_ready, exp_done, probs_ready = (
            sem(s) for s in ("scores_done", "max_ready", "exp_done", "probs_ready"))
        turned, pt_ready, att_done, post_done, tanh_done = (
            sem(s) for s in ("turned", "pt_ready", "att_done", "post_done", "tanh_done"))
        p6_copied, pool_h_ready = sem("p6_copied"), sem("pool_h_ready")
        bfg_loaded, fg_ready, fg_half, fg_exp, fg_ln, fc_ready, fc_stored, fq_turned, fq_ready = (
            sem(s) for s in ("bfg_loaded", "fg_ready", "fg_half", "fg_exp", "fg_ln", "fc_ready", "fc_stored",
                             "fq_turned", "fq_ready"))
        x_loaded, h_ready, h_stored, h_loaded, out_stored = (
            sem(s) for s in ("x_loaded", "h_ready", "h_stored", "h_loaded", "out_stored"))
        dve_seq, pool_seq = sem("dve_seq"), sem("pool_seq")

        block = ctx.enter_context(nc.Block())

        def wait(e, s, value):
            if not isinstance(value, int) or value > 0:
                e.wait_ge(s, value)

        class Steps:

            def __init__(self, e, s):
                self.e, self.s, self.start, self.k = e, s, 0, 0

            def mark(self, ins):
                ins.then_inc(self.s, 1)
                self.k += 1

            def sync(self):
                self.e.wait_ge(self.s, self.start + self.k)

            def link(self, ins):
                self.mark(ins)
                self.sync()

            def loop(self, first, last, per, body):
                start = self.start + self.k
                with self.e.Fori(first, last - 1, 2) as i:
                    for j in (0, 1):
                        self.start, self.k = i * per + (start + (j - first) * per), 0
                        body(i + j, j)
                        assert self.k == per, (self.k, per)
                self.start, self.k = start + (last - first) * per, 0

        def pairs(e, first, last, body):
            with e.Fori(first, last - 1, 2) as i:
                for j in (0, 1):
                    body(i + j, j)

        def half(i, j):
            return (i - j) * 8 if not isinstance(i, int) else (i // 2) * 16

        def mem_tiles_at(n):
            return range(3 * n, min(3 * n + 3, KD))

        def x_tiles_at(n):
            return range(n, n + 1) if n < 8 else range(min(2 * n - 8, KD), min(2 * n - 6, KD))

        def joined(u):
            return 3 + 2 * u

        def joined_main(g):
            return g + (min(max(g - 2, 0), MEMH) if isinstance(g, int) else MEMH)

        @block.sync
        def _(sp):
            def load(n, slot, src, width=KD * P):
                wait(sp, lo_done, 2 * (n - 1))
                sp.dma_start(raw[slot][:, :width], src).then_inc(raw_loaded[slot], 16)

            def loads(base, first, last, src, width=KD * P):
                pairs(sp, first, last, lambda m, j: load(base + m, (base + j) % 2, src(m), width))

            load(N_MEM, 0, w_mem[0])
            sp.wait_ge(cols_loaded, 16)
            load(N_MEM + 1, 1, w_mem[1])
            loads(N_MEM, 2, 16, lambda m: w_mem[m])
            loads(N_INA, 0, 14, lambda m: w_in_a[m])

            def ublk_load(b, j):
                src = proj_a[b].rearrange("(g h) (t c) -> h t g c", g=GB, t=TC)
                sp.dma_start(ublk[:, j, :, :], src.rearrange("h t g c -> (h t) g c")).then_inc(ublk_loaded[j], 16)

            def batch_loads(b, j):
                sp.wait_ge(g_ready, b + 1)
                sp.dma_start(lag_s[j], lagpad[:].rearrange("p l h -> p (l h)")).then_inc(lag_stored, 16)
                sp.wait_ge(lag_stored, (b + 1) * 16)
                lag_rows = lag_s[j].rearrange("(g h) c -> h g c", g=GB)
                for t in range(TC):
                    sp.dma_start(toep[t:P:TC, j, :, :], lag_rows[:, :, (TC - 1 - t) * 16:(TC - 1 - t) * 16 + P]
                                 ).then_inc(toep_loaded[j], 16)

            sp.wait_ge(region_clear, 1)
            sp.wait_ge(stage_stored[0], 16 * 9)
            ublk_load(0, 0)

            def batch_step(b, j):
                last = isinstance(b, int) and b == 11
                if not last:
                    sp.wait_ge(params_ready, b + 1)
                    sp.dma_start(bcp[:, :, :], bc_d[b + 1]).then_inc(bc_loaded, 16)
                load(N_INA + 14 + b, j, w_in_a[14 + b])
                batch_loads(b, j)
                if last:
                    return
                wait(sp, ssm_y_done, b)
                sp.wait_ge(stage_stored[1 - j], b * 8 + 16 * 9 + 8 * j)
                ublk_load(b + 1, 1 - j)

            batch_step(0, 0)
            batch_step(1, 1)
            pairs(sp, 2, 10, batch_step)
            batch_step(10, 0)
            batch_step(11, 1)
            def yu_load(m, slot):
                for g in range(GB):
                    sp.dma_start(ym[16 * g:16 * g + 16, slot, :].rearrange("h (t c) -> h t c", t=TC),
                                 y_s[m, g].rearrange("(t h) c -> h t c", t=TC)).then_inc(yu_loaded[slot], 16)
                sp.dma_start(um[:, slot, :], proj_a[m]).then_inc(yu_loaded[slot], 16)

            load(N_INA + 26, 0, w_in_a[26])
            load(N_INA + 27, 1, w_in_a[27])
            sp.wait_ge(y_stored, 16 * NB)
            sp.wait_ge(rot_done, NB)
            yu_load(0, 0)
            yu_load(1, 1)

            def gelu_step(i, j, src, width=KD * P):
                load(N_INA + 28 + i, j, src, width)
                for slot in (0, 1):
                    sp.wait_ge(yv_ready, i * 2 + slot + 1)
                    yu_load(i * 2 + slot + 2, slot)

            pairs(sp, 0, 4, lambda i, j: gelu_step(i, j, w_in_a[28 + i]))
            gelu_step(4, 0, w_glu[0], HEADS * P)
            load(N_GLU + 1, 1, w_glu[1], HEADS * P)

            def memory_head_load(u):
                for dst, src in ((q_a, proj_a[24 + u]), (k_a, mem_s[u]), (v_a, mem_s[MEMH + u])):
                    sp.dma_start(dst[:, u, :], src).then_inc(mq_loaded[u], 16)

            sp.wait_ge(yg_done, HEADS)
            sp.wait_ge(stage_stored[0], 16 * 22)
            sp.wait_ge(stage_stored[1], 16 * 22)
            for g in range(2):
                sp.dma_start(z_a[:, g, :], proj_a[12 + g]).then_inc(z_loaded[g], 16)
                memory_head_load(g)
            load(N_GLU + 2, 0, w_glu[2], HEADS * P)
            memory_head_load(2)
            memory_head_load(3)
            load(N_GLU + 3, 1, w_glu[3], HEADS * P)
            loads(N_GLU, 4, 12, lambda m: w_glu[m], HEADS * P)
            loads(N_OUTA, 0, 16, lambda m: w_out[0, m])
            loads(N_KV, 0, 24, lambda m: w_kv[m])
            load(N_FG, N_FG % 2, w_fg[0])

            loads(N_INB, 0, 16, lambda m: w_in_b[m])

            def qk_load(t, j, memory):
                wait(sp, scores_done, MEMH + t - 1)
                sp.dma_start(q_b[:, j, :], proj_b[t]).then_inc(qk_loaded[j], 16)
                if memory:
                    sp.dma_start(k_b[:, j, 0:NM], mem_s[t - HEADS + 2 * MEMH]).then_inc(qk_loaded[j], 16)
                else:
                    sp.dma_start(k_b[:, j, :], kv_s[t]).then_inc(qk_loaded[j], 16)
                    wait(sp, max_ready, MEMH + t - 1)
                    fc_row = fc_s[t:t + 1, :] if isinstance(t, int) else fc_s[bass.ds(t, 1), :]
                    sp.dma_start(bias_b[:, j, :], fc_row.partition_broadcast(P)).then_inc(qk_loaded[j], 16)

            def v_load(t, j, memory):
                wait(sp, att_done, MEMH + t - 1)
                if memory:
                    sp.dma_start(v_b[:, j, 0:NM], mem_s[t - HEADS + 3 * MEMH]).then_inc(v_loaded[j], 16)
                else:
                    sp.dma_start(v_b[:, j, :], kv_s[t + HEADS]).then_inc(v_loaded[j], 16)

            def unit_step(t, j, memory, memory_v):
                load(N_INB + 16 + t, (N_INB + j) % 2, w_in_b[16 + t])
                qk_load(t, j, memory)
                if not isinstance(t, int) or t >= 2:
                    v_load(t - 2, j, memory_v)

            sp.wait_ge(fc_stored, 16)
            sp.wait_ge(h_ready, 16)
            sp.wait_ge(stage_stored[0], 16 * 37)
            sp.wait_ge(stage_stored[1], 16 * 37)
            unit_step(0, 0, False, False)
            unit_step(1, 1, False, False)
            sp.wait_ge(stage_stored[0], 16 * 44)
            sp.wait_ge(stage_stored[1], 16 * 44)
            pairs(sp, 2, 12, lambda t, j: unit_step(t, j, False, False))
            unit_step(12, 0, True, False)
            unit_step(13, 1, True, False)
            unit_step(14, 0, True, True)
            unit_step(15, 1, True, True)
            load(N_OUTB, N_OUTB % 2, w_out[1, 0])
            v_load(14, 0, True)
            load(N_OUTB + 1, (N_OUTB + 1) % 2, w_out[1, 1])
            v_load(15, 1, True)
            loads(N_OUTB, 2, 16, lambda m: w_out[1, m])
            sp.wait_ge(act_lo_done, 96)
            sp.dma_start(h_t[:, :, :], h_s.rearrange("k p t -> p k t")).then_inc(h_loaded, 16)
            for first, last, done, count in ((0, 4, h_ready, 20), (TAIL, TAIL + 2, pool_h_ready, 2), (4, 8, h_ready, 24),
                                             (TAIL + 2, 16, pool_h_ready, 16 - TAIL), (8, TAIL, h_ready, 16 + TAIL)):
                sp.wait_ge(done, count)
                sp.dma_start(out_t[first:last].rearrange("k p t -> p k t"), h_t[:, first:last, :]).then_inc(out_stored, 16)
            sp.wait_ge(out_stored, 80)

        @block.gpsimd
        def _(pool):
            nc.gpsimd.memset(ones[:, :], 1.0).then_inc(consts_ready, 1)
            nc.gpsimd.memset(ident[:, :], 0.0).then_inc(consts_ready, 1)
            nc.gpsimd.memset(mask[:, :], 0.0).then_inc(consts_ready, 1)
            nc.gpsimd.memset(c_half_pi, HALF_PI).then_inc(consts_ready, 1)
            nc.gpsimd.memset(c_sgn, -1.0).then_inc(consts_ready, 1)
            nc.gpsimd.memset(c_nsgn, 1.0).then_inc(consts_ready, 1)
            nc.gpsimd.memset(c_one, 1.0).then_inc(consts_ready, 1)
            pool.wait_ge(consts_ready, 7)
            nc.gpsimd.memset(consts[64:P, 1:2], 1.0).then_inc(consts_ready, 1)
            nc.gpsimd.memset(consts[64:P, 2:3], -1.0).then_inc(consts_ready, 1)
            pool.wait_ge(consts_ready, 9)
            nc.gpsimd.affine_select(out=ident[:, :], in_=ident[:, :], compare_op=ALU.not_equal, fill=1.0, base=0,
                                    pattern=[[-1, P]], channel_multiplier=1).then_inc(consts_ready, 1)
            nc.gpsimd.affine_select(out=mask[:, :], in_=mask[:, :], compare_op=ALU.is_ge, fill=MASKED, base=0,
                                    pattern=[[-1, P]], channel_multiplier=1).then_inc(consts_ready, 1)

            def low(n, slot):
                for h, k in enumerate((slice(0, KD // 2), slice(KD // 2, KD))):
                    pool.wait_ge(hi_done, 2 * n + h + 1)
                    nc.gpsimd.tensor_tensor(w_lo[slot][:, k, :], raw[slot][:, :].rearrange("p (k m) -> p k m", k=KD)[:, k, :],
                                            w_hi[slot][:, k, :].bitcast(F32), ALU.subtract).then_inc(lo_done, 1)

            pairs(pool, 0, 18, low)
            pool.wait_ge(gemm_done, 16)
            pool.wait_ge(vstaged, 8)
            pool.wait_ge(r_ready, 2)
            nc.gpsimd.memset(x1[:, :, :], 0.0)
            nc.gpsimd.memset(x2[:, :, :], 0.0)
            nc.gpsimd.memset(lagpad[:, :, :], 0.0)
            nc.gpsimd.memset(bdiag[:, :], 0.0)
            nc.gpsimd.iota(cidx[:, :], pattern=[[1, NC]], base=0, channel_multiplier=0,
                           allow_small_or_imprecise_dtypes=True).then_inc(region_clear, 1)
            pairs(pool, 18, N_KV + 2, low)

            pool.wait_ge(sq_ready, 49)
            nc.gpsimd.tensor_copy(acc1[:, :], sq1[:, 0, :]).then_inc(sq_used, 1)

            def total(k, slot):
                pool.wait_ge(sq_ready, 49 + k)
                pool.wait_ge(sq_used, 48 + k)
                nc.gpsimd.tensor_tensor(acc1[:, :], acc1[:, :], sq1[:, slot, :], ALU.add).then_inc(sq_used, 1)

            total(1, 1)
            pairs(pool, 2, 16, total)
            pairs(pool, N_KV + 2, N_BLOCKS - 1, low)
            low(N_BLOCKS - 1, (N_BLOCKS - 1) % 2)

            pool.wait_ge(r_ready, 5)
            pool.wait_ge(h_loaded, 16)
            pool.wait_ge(out_taken, N_BLOCKS)
            for k in range(TAIL, KD):
                nc.gpsimd.tensor_tensor(o_t[:, k, :], o_t[:, k, :], rbc[:, :], ALU.mult).then_inc(pool_seq, 1)
                pool.wait_ge(pool_seq, k - TAIL + 1)
                nc.gpsimd.tensor_tensor(h_t[:, k, :], h_t[:, k, :], o_t[:, k, :], ALU.add).then_inc(pool_h_ready, 1)

        @block.tensor
        def _(pe):
            def split_ready(n, halves):
                pe.wait_ge(hi_done, 2 * n + halves)
                pe.wait_ge(lo_done, 2 * n + halves)

            def product(slot, k, hi, lo, width, first, last):
                out = pgemm[:, slot, 0:width]
                pe.matmul(out, w_hi[slot][:, k, :], hi[:, k, :], start=first, stop=False)
                pe.matmul(out, w_hi[slot][:, k, :], lo[:, k, :], start=False, stop=False)
                return pe.matmul(out, w_lo[slot][:, k, :], hi[:, k, :], start=False, stop=last)

            def gemm(n, slot, hi, lo, kt=KD, width=T, splits=None, order=None, split_done=act_lo_done, halfway=None,
                     half_done=None):
                split_ready(n, 1 if order is None else 2)
                wait(pe, out_taken, n - 1)
                for i, k in enumerate(order or range(kt)):
                    if splits is not None:
                        pe.wait_ge(split_done, splits + i + 1)
                    if i == kt // 2 and halfway is not None:
                        halfway()
                    if i == KD // 2 and order is None:
                        split_ready(n, 2)
                    last = product(slot, k, hi, lo, width, i == 0, i == kt - 1)
                    if half_done is not None and i == kt // 2 - 1:
                        last.then_inc(half_done, 1)
                last.then_inc(gemm_done, 1)

            def joint_blocks(n, hi, lo, splits, sums, width=T):
                wait(pe, out_taken, n)
                for i in range(KD + LAG):
                    for slot, k in ((0, i), (1, i - LAG)):
                        if not 0 <= k < KD:
                            continue
                        if k % (KD // 2) == 0:
                            split_ready(n + slot, 1 + k // (KD // 2))
                        if slot == 0:
                            pe.wait_ge(act_lo_done, splits + k + 1)
                        last = product(slot, k, hi, lo, width, k == 0, k == KD - 1)
                        if k == KD - 1:
                            last.then_inc(gemm_done, 1)
                    if i == KD + 1:
                        sums()

            def blocks(base, first, last, kt=KD, hi=act_hi, lo=act_lo):
                pairs(pe, first, last, lambda m, j: gemm(base + m, (base + j) % 2, hi, lo, kt))

            def stat(e, acc, width=T):
                pe.wait_ge(sq_used, 16 * (e + 1))
                for i in range(width // P):
                    last = pe.matmul(p7[:, i:i + 1], acc[:, i * P:(i + 1) * P], ones[:, 0:1], start=(i == 0), stop=True,
                                     skip_group_check=True)
                last.then_inc(stat_done, 1)

            def spread(e, diag, width=T):
                pe.wait_ge(diag_ready, e + 1)
                pe.matmul(p7[:, 0:width], ones[:, :], diag[:, 0:width], start=True, stop=True).then_inc(spread_done, 1)

            def turn_values(c, n, vt, slot, tiles):
                pe.wait_ge(out_taken, n + 1)
                wait(pe, vstaged, c)
                for i in range(tiles):
                    last = pe.transpose(pt[:, i * P:(i + 1) * P], vt[:, slot, i * P:(i + 1) * P], ident[:, :])
                last.then_inc(vturned, 1)

            pe.wait_ge(consts_ready, 11)
            def memory_turn(n):
                c = 4 * (n // 8) + n % 4
                turn_values(c, n, vt0, n % 2, 2)

            joint_blocks(N_MEM, mact_hi[:, 0], mact_lo[:, 0], 0, lambda: stat(0, acc0, NM), NM)
            spread(0, diag0, NM)
            for n in range(2, 4 * MEMH):
                if n == 8:
                    pe.wait_ge(mem_lo_done, KD)
                value_before = (n - 1) % 8 >= MEMH
                gemm(n, n % 2, mact_hi[:, n // 8], mact_lo[:, n // 8], KD, NM,
                     halfway=(lambda: memory_turn(n - 1)) if value_before else None)

            stat(1, acc0)
            def last_turn():
                memory_turn(N_INA - 1)
                spread(1, diag0)

            gemm(N_INA, 0, act_hi, act_lo, splits=16, halfway=last_turn)
            gemm(N_INA + 1, 1, act_hi, act_lo)
            blocks(N_INA, 2, 12)

            def group_params(b, j):
                pe.wait_ge(params_ready, b + 1)
                wait(pe, g_ready, b)
                for g in range(GB):
                    pe.transpose(pt[:, g * P:(g + 1) * P], gst[:, g, :, :].rearrange("p h t -> p (h t)"), ident[:, :])
                for g in range(GB):
                    last = pe.matmul(p7[:, 0:P], bdiag[:, g * P:(g + 1) * P],
                                     hc[:, j, g, 0:TC, :].rearrange("p l h -> p (l h)"),
                                     start=(g == 0), stop=(g == GB - 1))
                last.then_inc(lags_done, 1)

            def group_states(b, j):
                pe.wait_ge(g_ready, b + 1)
                pe.wait_ge(ublk_loaded[j], half(b, j) + 16)
                wait(pe, rot_done, b)
                for g in range(GB):
                    cols_g = slice(g * NC, (g + 1) * NC)
                    pe.matmul(ps[:, 0, cols_g], g1[:, g, :], ublk[:, j, g, :], start=True, stop=True)
                    last = pe.matmul(ps[:, 1, cols_g], g2[:, g, :], ublk[:, j, g, :], start=True, stop=True)
                last.then_inc(states_done, 1)

            def group_outputs(b, j):
                pe.wait_ge(rot_done, b + 1)
                pe.wait_ge(toep_loaded[j], (half(b, j) + 16) * TC)
                wait(pe, y_taken, b)
                for g in range(GB):
                    out = p6[:, g * NC:(g + 1) * NC]
                    pe.matmul(out, toep[:, j, g, :], ublk[:, j, g, :], start=True, stop=False)
                    pe.matmul(out, hc[:, j, g, 1:TC + 1, :].rearrange("p l h -> p (l h)"), x1[:, g, :],
                              start=False, stop=False)
                    last = pe.matmul(out, hrot[:, j, g, :, :].rearrange("p l h -> p (l h)"), x2[:, g, :],
                                     start=False, stop=True)
                last.then_inc(ssm_y_done, 1)

            def batch(b, j):
                group_params(b, j)
                before = not isinstance(b, int) or b > 0
                gemm(N_INA + 12 + b, j, act_hi, act_lo,
                     halfway=(lambda: group_outputs(b - 1, 1 - j)) if before else None)
                group_states(b, j)

            batch(0, 0)
            batch(1, 1)
            pairs(pe, 2, 12, batch)
            gemm(N_INA + 24, 0, act_hi, act_lo, halfway=lambda: group_outputs(11, 1))
            gemm(N_INA + 25, 1, act_hi, act_lo)
            blocks(N_INA, 26, 32)

            def mem_scores(u, q, k):
                wait(pe, max_ready, u)
                for i in range(4):
                    last = pe.matmul(ps[:, i // 2, (i % 2) * NM:(i % 2 + 1) * NM], q[:, i * P:(i + 1) * P], k,
                                     start=(i % 2 == 0), stop=True, skip_group_check=True)
                last.then_inc(scores_done, 1)

            def mem_turn(u, s):
                pe.wait_ge(probs_ready, u + 1)
                wait(pe, pt_ready, u)
                for m in range(2):
                    for i in range(4):
                        last = pe.transpose(pt[:, m * T + i * P:m * T + (i + 1) * P], s[:, i, m * P:(m + 1) * P],
                                            ident[:, :])
                last.then_inc(turned, 1)

            def mem_values(u, v, p_t):
                pe.wait_ge(pt_ready, u + 1)
                for m in range(2):
                    last = pe.matmul(p7[:, :], v[:, m * P:(m + 1) * P], p_t[:, m, :], start=(m == 0), stop=(m == 1))
                last.then_inc(att_done, 1)

            def next_head(u):
                if u > 0:
                    mem_turn(u - 1, s_a)
                if u < MEMH:
                    pe.wait_ge(mq_loaded[u], 48)
                    mem_scores(u, q_a[:, u, :], k_a[:, u, :])

            gemm(N_GLU, 0, yg_hi, yg_lo, HEADS, splits=0, split_done=yg_done)
            for u in range(MEMH + 1):
                gemm(N_GLU + 1 + u, (1 + u) % 2, yg_hi, yg_lo, HEADS, halfway=lambda: next_head(u))
                if u > 0:
                    if u > 1:
                        pe.wait_ge(main_ready, joined(u - 2) + 1)
                    mem_values(u - 1, v_a[:, u - 1, :], p_a)
            blocks(N_GLU, 6, 12, HEADS, yg_hi, yg_lo)

            made = sorted(range(KD), key=lambda k: joined_main(k) if k < HEADS else joined(k - HEADS))
            gemm(N_OUTA, 0, act_hi, act_lo, splits=32, order=made)
            gemm(N_OUTA + 1, 1, act_hi, act_lo)
            blocks(N_OUTA, 2, 16)
            stat(2, acc1)
            spread(2, diag1)
            joint_blocks(N_KV, act_hi, act_lo, 48, lambda: stat(3, acc1))
            spread(3, diag1)
            blocks(N_KV, 2, 12)
            gemm(N_KV + 12, 0, act_hi, act_lo)

            def value_block(m, j):
                gemm(N_KV + 12 + m, j, act_hi, act_lo,
                     halfway=lambda: turn_values(m + 7, N_KV + 11 + m, vt1, 1 - j, 4))

            value_block(1, 1)
            pairs(pe, 2, 12, value_block)
            gemm(N_FG, N_FG % 2, act_hi, act_lo, half_done=fg_half,
                 halfway=lambda: turn_values(19, N_KV + 23, vt1, 1, 4))

            gemm(N_INB, 1, act_hi, act_lo, splits=64)
            gemm(N_INB + 1, 0, act_hi, act_lo)
            pe.wait_ge(fc_ready, 1)
            pe.wait_ge(vstaged, 20)
            for i in range(4):
                last = pe.transpose(pt[:, i * HEADS:(i + 1) * HEADS], fgb[0:HEADS, i * P:(i + 1) * P],
                                    ident[0:HEADS, 0:HEADS])
            last.then_inc(fq_turned, 1)
            blocks(N_INB, 2, 16)

            def fox_scores(t, j):
                wait(pe, max_ready, MEMH + t)
                q, k = q_b[:, j, :], k_b[:, j, :]
                first = dict(start=True, stop=True, skip_group_check=True)
                more = dict(start=False, stop=True, skip_group_check=True)
                pe.matmul(ps[:, 0, 0:P], q[:, 0:P], k[:, 0:P], **first)
                pe.matmul(ps[:, 0, P:4 * P], q[:, 2 * P:3 * P], k[:, 0:3 * P], **more)
                pe.matmul(ps[:, 1, :], q[:, 3 * P:4 * P], k, **first)
                wait(pe, p6_copied, t)
                pe.matmul(p6[:, 0:2 * P], q[:, P:2 * P], k[:, 0:2 * P], **first).then_inc(scores_done, 1)

            def fox_turn(t):
                pe.wait_ge(probs_ready, MEMH + t + 1)
                pe.wait_ge(pt_ready, MEMH + t)
                for i, out in ((3, pt[:, 0:T]), (2, pt[:, T:T + 3 * P]), (0, pt[:, T + 3 * P:2 * T]), (1, p6[:, 2 * P:T])):
                    for k in range(i + 1):
                        last = pe.transpose(out[:, k * P:(k + 1) * P], s_b[:, i, k * P:(k + 1) * P], ident[:, :])
                last.then_inc(turned, 1)

            def fox_values(t, j):
                pe.wait_ge(pt_ready, MEMH + t + 1)
                pe.wait_ge(v_loaded[j], half(t, j) + 16)
                wait(pe, post_done, t)
                for k in range(4):
                    last = pe.matmul(p7[:, k * P:T], v_b[:, j, k * P:(k + 1) * P], pt_b[:, k, k * P:T],
                                     start=(k == 0), stop=(k == 3), skip_group_check=True)
                last.then_inc(att_done, 1)

            def fox(t, j):
                pe.wait_ge(qk_loaded[j], half(t, j) * 3 + 48)
                fox_scores(t, j)
                gemm(N_INB + 16 + t, (N_INB + j) % 2, act_hi, act_lo)
                if not isinstance(t, int) or t > 0:
                    fox_values(t - 1, 1 - j)
                fox_turn(t)

            fox(0, 0)
            fox(1, 1)
            pairs(pe, 2, 12, fox)
            for t in range(HEADS, UNITS):
                j = t % 2
                pe.wait_ge(qk_loaded[j], 16 * (18 + 2 * ((t - HEADS) // 2 + 1)))
                mem_scores(MEMH + t, q_b[:, j, :], k_b[:, j, 0:NM])
                gemm(N_INB + 16 + t, (N_INB + j) % 2, act_hi, act_lo)
                if t == HEADS:
                    fox_values(t - 1, 1 - j)
                else:
                    pe.wait_ge(v_loaded[1 - j], 16 * ((t - 1) // 2 + 1))
                    pe.wait_ge(post_done, t - 1)
                    mem_values(MEMH + t - 1, v_b[:, 1 - j, :], pt_b)
                mem_turn(MEMH + t, s_b)
            pe.wait_ge(v_loaded[1], 16 * 8)
            pe.wait_ge(post_done, UNITS - 1)
            mem_values(MEMH + 15, v_b[:, 1, :], pt_b)

            gemm(N_OUTB, 1, act_hi, act_lo, splits=80)
            gemm(N_OUTB + 1, 0, act_hi, act_lo)
            blocks(N_OUTB, 2, 16)
            stat(4, acc1)
            spread(4, diag1)

        @block.scalar
        def _(act):
            def high(n, slot):
                wait(act, gemm_done, n - 1)
                act.wait_ge(raw_loaded[slot], half(n, slot) + 16)
                for k in (slice(0, KD // 2), slice(KD // 2, KD)):
                    act.activation(w_hi[slot][:, k, :], raw[slot][:, :].rearrange("p (k m) -> p k m", k=KD)[:, k, :],
                                   ACT.Copy).then_inc(hi_done, 1)

            def store(n, s, slot, dst):
                act.wait_ge(out_taken, n + 1)
                act.dma_start(dst, stage[:, slot, :]).then_inc(stage_stored[slot], 16)

            def value_out(c, s, slot, width, dst):
                act.wait_ge(vturned, c + 1)
                wait(act, stage_stored[slot], half(s, slot))
                act.activation(stage[:, slot, 0:width], pt[:, 0:width], ACT.Copy).then_inc(vstaged, 1)
                act.wait_ge(vstaged, c + 1)
                act.dma_start(dst, stage[:, slot, 0:width]).then_inc(stage_stored[slot], 16)

            def square(q, slot, src, sq):
                wait(act, sq_used, q - 1)
                act.activation(sq[:, slot, 0:src.shape[-1]], src, ACT.Square).then_inc(sq_ready, 1)

            def deviation(e, cols_used=4):
                act.wait_ge(var_ready, e + 1)
                act.activation(dev[:, 0:cols_used], var[:, 0:cols_used], ACT.Sqrt).then_inc(dev_ready, 1)

            act.dma_start(cols[:, :], cols_d).then_inc(cols_loaded, 16)
            for g in range(4):
                act.dma_start(mem_raw[:, 4 * g:4 * g + 4, :],
                              mem_t[4 * g:4 * g + 4].rearrange("k p t -> p k t")).then_inc(mem_loaded[g], 16)

            def x_load(k, slot):
                act.dma_start(xs[:, slot, :], x_t[k]).then_inc(xs_loaded[slot], 16)

            x_load(0, 0)
            x_load(1, 1)
            act.wait_ge(cols_loaded, 16)
            high(0, 0)
            for k in range(KD):
                if k % 4 == 0:
                    act.wait_ge(mem_loaded[k // 4], 16)
                if k == 9:
                    high(1, 1)
                act.activation(mact_hi[:, 0, k, :], mem_raw[:, k, :], ACT.Identity,
                               scale=cols[:, C_MEMG + k:C_MEMG + k + 1]).then_inc(act_hi_done, 1)
                square(k, k % 2, mem_raw[:, k, :], sq0)

            def mem_tile(k):
                c = C_MEMG + KD + k
                act.activation(mact_hi[:, 1, k, :], mem_raw[:, k, :], ACT.Identity,
                               scale=cols[:, c:c + 1]).then_inc(mem_hi_done, 1)

            def x_tile(k, slot):
                act.wait_ge(xs_loaded[slot], half(k, slot) + 16)
                act.activation(act_hi[:, k, :], xs[:, slot, 0:T], ACT.Identity,
                               scale=cols[:, bass.ds(C_PRE + k, 1)]).then_inc(act_hi_done, 1)
                square(16 + k, slot, xs[:, slot, 0:T], sq0)
                if not isinstance(k, int) or k < 14:
                    act.wait_ge(sq_ready, 17 + k)
                    act.wait_ge(act_lo_done, 17 + k)
                    x_load(k + 2, slot)

            def memory_out(n):
                value_out(4 * (n // 8) + n % 4, n, n % 2, NM, mem_s[n])

            for n in range(16):
                if n == 0:
                    deviation(0, 2)
                high(n + 2, n % 2)
                if n > 0 and (n - 1) % 8 >= MEMH:
                    memory_out(n - 1)
                if n % 8 < MEMH:
                    act.wait_ge(out_taken, n + 1)
                    act.dma_start(mem_s[n], stage[:, n % 2, 0:NM]).then_inc(stage_stored[n % 2], 16)
                for k in mem_tiles_at(n):
                    mem_tile(k)
                for k in x_tiles_at(n):
                    x_tile(k, k % 2)

            deviation(1)
            memory_out(15)

            def u_block(m, j):
                high(N_INA + m + 2, j)
                store(N_INA + m, 16 + m, j, proj_a[m])

            u_block(0, 0)
            u_block(1, 1)
            act.wait_ge(region_clear, 1)
            act.dma_start(tB[:, 0:3 * GROUPS], lam_d).then_inc(lam_loaded, 16)
            act.dma_start(bcp[:, :, :], bc_d[0]).then_inc(bc_loaded, 16)
            pairs(act, 2, 4, u_block)
            act.wait_ge(sin_asked, 1)
            act.activation(bco[:, 0, :], bco[:, 0, :], ACT.Sin).then_inc(sin_done, 1)
            act.activation(bco[:, 1, :], bco[:, 1, :], ACT.Sin, scale=0.5).then_inc(sin_done, 1)
            pairs(act, 4, 12, u_block)

            def batch(b, j):
                act.wait_ge(phase_ready, b + 1)
                act.activation(sin_t[:, :], tB[:, :], ACT.Sin, scale=-TWO_PI)
                act.activation(cos_t[:, :], tA[:, 0:T], ACT.Sin, scale=-TWO_PI, bias=c_half_pi).then_inc(trig_done, 1)
                act.wait_ge(lags_done, b + 1)
                wait(act, states_done, b)
                wait(act, lag_stored, b * 16)
                ptg = pt[:, :].rearrange("p (g s) -> p g s", g=GB)
                act.activation(g1[:, :, :], ptg, ACT.Copy)
                act.activation(g2[:, :, 0:64], ptg[:, :, 64:P], ACT.Copy)
                act.activation(g2[:, :, 64:P], ptg[:, :, 0:64], ACT.Copy, scale=-1.0)
                act.activation(lagpad[:, TC - 1:, :], p7[:, 0:P].rearrange("p (l h) -> p l h", l=TC),
                               ACT.Copy).then_inc(g_ready, 1)
                if not isinstance(b, int) or b > 0:
                    y_out(b - 1)
                high(N_INA + 14 + b, j)
                store(N_INA + 12 + b, 28 + b, j, proj_a[12 + b])

            def y_out(b):
                act.wait_ge(ssm_y_done, b + 1)
                wait(act, y_stored, b * 16)
                act.activation(ystage[:, :], p6[:, :], ACT.Copy).then_inc(y_taken, 1)
                act.wait_ge(y_taken, b + 1)
                act.dma_start(y_s[b].rearrange("g q c -> q g c"),
                              ystage[:, :].rearrange("p (g c) -> p g c", g=GB)).then_inc(y_stored, 16)

            batch(0, 0)
            batch(1, 1)
            pairs(act, 2, 12, batch)
            high(N_INA + 26, 0)
            store(N_INA + 24, 40, 0, proj_a[24])
            y_out(11)
            high(N_INA + 27, 1)
            store(N_INA + 25, 41, 1, proj_a[25])

            def gelu_block(i, j):
                for slot in (0, 1):
                    m = i * 2 + slot
                    act.wait_ge(yv_ready, m + 1)
                    act.activation(yq[:, slot, :], yv[:, slot, :], ACT.Square).then_inc(ysq_done, 1)
                for slot in (0, 1):
                    act.wait_ge(yin_ready, i * 2 + slot + 1)
                    act.activation(yth[:, slot, :], yq[:, slot, :], ACT.Tanh, scale=GELU_C).then_inc(yth_done, 1)
                for slot in (0, 1):
                    m = i * 2 + slot
                    act.wait_ge(yg_ready, m + 1)
                    act.activation(yg_hi[:, m, :], yv[:, slot, :], ACT.Copy, scale=0.5).then_inc(yghi_done, 1)
                high(N_INA + 28 + i, j)
                store(N_INA + 26 + i, 42 + i, j, proj_a[26 + i])

            pairs(act, 0, 6, gelu_block)

            def exps(u, s, widths):
                act.wait_ge(max_ready, u + 1)
                for i, w in enumerate(widths):
                    last = act.activation(s[:, i, 0:w], s[:, i, 0:w], ACT.Exp,
                                          bias=nmax[:, i:i + 1], accum_out=rsum[:, i:i + 1])
                last.then_inc(exp_done, 1)

            def mem_pt(u, p_t):
                act.wait_ge(turned, u + 1)
                wait(act, att_done, u)
                for m in range(2):
                    last = act.activation(p_t[:, m, :], pt[:, m * T:(m + 1) * T], ACT.Copy)
                last.then_inc(pt_ready, 1)

            def z_load(g, slot):
                act.dma_start(z_a[:, slot, :], proj_a[12 + g]).then_inc(z_loaded[slot], 16)

            def zm_load(u):
                act.dma_start(zm_a[:, :], proj_a[28 + u]).then_inc(zm_loaded, 16)

            def gate_block(g, j, last_two=False):
                n, c = N_GLU + g, joined_main(g)
                unit = g - 1 if isinstance(g, int) and 1 <= g <= MEMH else None
                after = g - 2 if isinstance(g, int) and 2 <= g <= MEMH + 1 else None
                if unit is not None:
                    exps(unit, s_a, [NM] * 4)
                wait(act, main_ready, c)
                act.wait_ge(z_loaded[j], half(g, j) + 16)
                act.activation(tz_a[:, :], z_a[:, j, :], ACT.Tanh, scale=0.5).then_inc(tz_done, 1)
                act.wait_ge(gemm_done, n + 1)
                act.activation(tg_a[:, :], pgemm[:, j, :], ACT.Tanh, scale=0.5,
                               bias=hbglu[:, bass.ds(g, 1)]).then_inc(out_taken, 1)
                high(n + 2, j)
                act.wait_ge(main_ready, c + 1)
                act.activation(act_hi[:, g, :], y2_a[:, :], ACT.Copy, scale=0.25).then_inc(act_hi_done, 1)
                if not last_two:
                    z_load(g + 2, j)
                if unit is not None:
                    mem_pt(unit, p_a)
                if after is not None:
                    act.wait_ge(zm_loaded, 16 * (after + 1))
                    act.activation(tz_a[:, :], zm_a[:, :], ACT.Tanh, scale=0.5).then_inc(tz_done, 1)
                    act.wait_ge(main_ready, c + 2)
                    act.activation(act_hi[:, HEADS + after, :], y2_a[:, :], ACT.Copy, scale=0.5).then_inc(act_hi_done, 1)
                    if after < MEMH - 1:
                        zm_load(after + 1)

            act.wait_ge(yg_done, HEADS)
            gate_block(0, 0)
            act.wait_ge(stage_stored[0], 16 * 24)
            act.wait_ge(stage_stored[1], 16 * 24)
            zm_load(0)
            for g in range(1, 6):
                gate_block(g, g % 2)
            pairs(act, 6, 10, gate_block)
            gate_block(10, 0, True)
            gate_block(11, 1, True)

            act.wait_ge(act_lo_done, 48)
            act.wait_ge(gemm_done, N_OUTA)
            act.dma_start(h_t[:, :, :], x_t.rearrange("k p t -> p k t")).then_inc(x_loaded, 16)

            def out_block(base, q, layer):
                def body(m, j, more=True):
                    slot = (base + j) % 2
                    act.wait_ge(gemm_done, base + m + 1)
                    square(q + m, j, pgemm[:, slot, :], sq1)
                    act.activation(o_t[:, m, :], pgemm[:, slot, :], ACT.Identity,
                                   scale=cols[:, bass.ds(C_POST + layer * KD + m, 1)]).then_inc(out_taken, 1)
                    if more:
                        high(base + m + 2, slot)
                return body

            out_a = out_block(N_OUTA, 32, 0)
            pairs(act, 0, 14, out_a)
            out_a(14, 0)
            out_a(15, 1, False)
            deviation(2)
            high(N_KV + 1, 1)

            def h_tile(k, j):
                act.wait_ge(sq_used, 47 + k)
                act.wait_ge(h_ready, k + 1)
                act.activation(act_hi[:, k, :], h_t[:, k, :], ACT.Identity,
                               scale=cols[:, bass.ds(C_KVG + k, 1)]).then_inc(act_hi_done, 1)
                act.activation(sq1[:, j, :], h_t[:, k, :], ACT.Square).then_inc(sq_ready, 1)

            pairs(act, 0, 16, h_tile)
            act.dma_start(h_s.rearrange("k p t -> p k t"), h_t[:, :, :]).then_inc(h_stored, 16)
            deviation(3)

            def k_block(m, j):
                high(N_KV + m + 2, j)
                store(N_KV + m, 48 + m, j, kv_s[m])

            pairs(act, 0, 12, k_block)

            def v_block(m, j):
                high(N_KV + 14 + m, j)
                value_out(m + 7, 59 + m, 1 - j, T, kv_s[m + 11])

            high(N_KV + 14, 0)
            high(N_KV + 15, 1)
            value_out(8, 60, 0, T, kv_s[12])
            pairs(act, 2, 12, v_block)
            value_out(19, 71, 1, T, kv_s[23])

            act.dma_start(fq[0:HEADS, 0, 0:1], bfg_d).then_inc(bfg_loaded, 16)

            def again(k, j):
                act.activation(act_hi[:, k, :], h_t[:, k, :], ACT.Identity,
                               scale=cols[:, bass.ds(C_PRE + KD + k, 1)]).then_inc(act_hi_done, 1)

            act.wait_ge(fg_half, 1)
            pairs(act, 0, KD // 2, again)
            high(N_FG + 2, 0)
            act.wait_ge(gemm_done, N_FG + 1)
            pairs(act, KD // 2, KD, again)
            act.wait_ge(fg_ready, 1)
            act.activation(fgb[0:HEADS, :], fgb[0:HEADS, :], ACT.Exp, scale=-1.0).then_inc(fg_exp, 1)
            act.wait_ge(fg_exp, 1)
            act.activation(fgb[0:HEADS, :], fgb[0:HEADS, :], ACT.Ln, bias=c_one[0:HEADS]).then_inc(fg_ln, 1)

            act.wait_ge(fc_ready, 1)
            act.dma_start(fc_s, fgb[0:HEADS, :]).then_inc(fc_stored, 16)

            def q_block(m, j):
                high(N_INB + m + 2, (N_INB + j) % 2)
                store(N_INB + m, 72 + m, j, proj_b[m])

            pairs(act, 0, 16, q_block)

            def unit(t, j, memory):
                u = MEMH + t
                exps(u, s_b, [NM] * 4 if memory else [P, 2 * P, 3 * P, 4 * P])
                high(N_INB + 18 + t, (N_INB + j) % 2)
                act.wait_ge(out_taken, N_INB + 17 + t)
                wait(act, post_done, t - 1)
                act.activation(sz_b[:, j, :], z_b[:, j, :], ACT.Tanh, scale=0.5).then_inc(tanh_done, 1)
                if memory:
                    mem_pt(u, pt_b)
                    return
                act.wait_ge(turned, u + 1)
                act.wait_ge(att_done, u)
                for i, out in ((1, p6[:, 2 * P:T]), (3, pt[:, 0:T]), (2, pt[:, T:T + 3 * P]), (0, pt[:, T + 3 * P:2 * T])):
                    last = act.activation(pt_b[:, 0:i + 1, i * P:(i + 1) * P],
                                          out.rearrange("p (k q) -> p k q", q=P), ACT.Copy)
                    if i == 1:
                        last.then_inc(p6_copied, 1)
                last.then_inc(pt_ready, 1)

            unit(0, 0, False)
            unit(1, 1, False)
            pairs(act, 2, 12, lambda t, j: unit(t, j, False))
            for t in range(HEADS, UNITS):
                unit(t, t % 2, True)

            def cat_tile(k, j):
                act.wait_ge(post_done, k + 1)
                act.activation(act_hi[:, k, :], cat_t[:, k, :], ACT.Copy).then_inc(act_hi_done, 1)

            act.wait_ge(gemm_done, N_OUTB)
            pairs(act, 0, 16, cat_tile)
            out_b = out_block(N_OUTB, 64, 1)
            act.wait_ge(act_lo_done, 96)
            pairs(act, 0, 14, out_b)
            out_b(14, 0, False)
            out_b(15, 1, False)
            deviation(4)

        @block.vector
        def _(dve):
            st = Steps(dve, dve_seq)
            tt, ts, stt = nc.vector.tensor_tensor, nc.vector.tensor_scalar, nc.vector.scalar_tensor_tensor

            def total(q, slot, acc, sq, width=T):
                dve.wait_ge(sq_ready, q + 1)
                if isinstance(q, int) and q % 16 == 0:
                    ins = nc.vector.tensor_copy(acc[:, 0:width], sq[:, slot, 0:width])
                else:
                    dve.wait_ge(sq_used, q)
                    ins = tt(acc[:, 0:width], acc[:, 0:width], sq[:, slot, 0:width], ALU.add)
                ins.then_inc(sq_used, 1)

            def inverse_rms(e, r, diag, width=T):
                n = width // P
                v, d, rc = var[:, 0:n], dev[:, 0:n], rcol[:, 0:n]
                dve.wait_ge(stat_done, e + 1)
                ts(v, p7[:, 0:n], 1.0 / D, EPS, ALU.mult, ALU.add).then_inc(var_ready, 1)
                dve.wait_ge(dev_ready, e + 1)
                st.link(nc.vector.reciprocal(rc, d))
                st.link(tt(d, rc, rc, ALU.mult))
                st.link(tt(d, d, v, ALU.mult))
                st.link(ts(d, d, -0.5, 1.5, ALU.mult, ALU.add))
                st.link(tt(rc, rc, d, ALU.mult))
                tt(diag[:, 0:width].rearrange("p (i q) -> p i q", q=P), rc.unsqueeze(2).broadcast_to([P, n, P]),
                   ident[:, :].unsqueeze(1).broadcast_to([P, n, P]), ALU.mult).then_inc(diag_ready, 1)
                dve.wait_ge(spread_done, e + 1)
                nc.vector.tensor_copy(r[:, 0:width], p7[:, 0:width]).then_inc(r_ready, 1)
                dve.wait_ge(r_ready, e + 1)

            def low(c, dst, src, col, hi):
                dve.wait_ge(act_hi_done, c + 1)
                if col is None:
                    ins = tt(dst, src, hi.bitcast(F32), ALU.subtract)
                else:
                    ins = stt(dst, src, col, hi.bitcast(F32), ALU.mult, ALU.subtract)
                ins.then_inc(act_lo_done, 1)

            def take(n, slot, s, stage_slot, out=None, source=None, by=None):
                dve.wait_ge(gemm_done, n + 1)
                if s is not None:
                    wait(dve, stage_stored[stage_slot], half(s, stage_slot))
                out = stage[:, stage_slot, :] if out is None else out
                source = pgemm[:, slot, :] if source is None else source
                tt(out, source, rbc[:, :] if by is None else by, ALU.mult).then_inc(out_taken, 1)

            dve.wait_ge(cols_loaded, 16)
            dve.wait_ge(consts_ready, 11)
            ts(hbglu[:, :], cols[:, C_BGLU:C_BGLU + HEADS], 0.5, None, ALU.mult)

            for k in range(KD):
                c = C_MEMG + k
                low(k, mact_lo[:, 0, k, :], mem_raw[:, k, :], cols[:, c:c + 1], mact_hi[:, 0, k, :])
                total(k, k % 2, acc0, sq0, NM)
            inverse_rms(0, rmem, diag0, NM)

            def x_tile(k, slot):
                low(16 + k, act_lo[:, k, :], xs[:, slot, :], cols[:, bass.ds(C_PRE + k, 1)], act_hi[:, k, :])
                total(16 + k, slot, acc0, sq0)

            for n in range(16):
                if n % 8 < MEMH:
                    take(n, n % 2, n, n % 2, stage[:, n % 2, 0:NM], pgemm[:, n % 2, 0:NM], rmem[:, :])
                else:
                    v = 4 * (n // 8) + n % 4
                    wait(dve, vturned, v - 1)
                    take(n, n % 2, None, None, vt0[:, n % 2, 0:NM], pgemm[:, n % 2, 0:NM], rmem[:, :])
                for k in mem_tiles_at(n):
                    c = C_MEMG + KD + k
                    dve.wait_ge(mem_hi_done, k + 1)
                    stt(mact_lo[:, 1, k, :], mem_raw[:, k, :], cols[:, c:c + 1], mact_hi[:, 1, k, :].bitcast(F32),
                        ALU.mult, ALU.subtract).then_inc(mem_lo_done, 1)
                for k in x_tiles_at(n):
                    x_tile(k, k % 2)
            inverse_rms(1, rbc, diag0)

            def u_block(m, j):
                def view(x):
                    return x.rearrange("p (c t) -> p c t", t=TC)
                take(N_INA + m, j, 16 + m, j, stage[:, j, :].rearrange("p (t c) -> p c t", t=TC),
                     view(pgemm[:, j, :]), view(rbc[:, :]))

            u_block(0, 0)
            u_block(1, 1)

            dve.wait_ge(lam_loaded, 16)
            la_re, la_im, step = (tB[:, i * GROUPS:(i + 1) * GROUPS] for i in range(3))
            tmp = [tA[:, i * GROUPS:(i + 1) * GROUPS] for i in range(12)]
            decay_i = decay[:, 0:GROUPS].bitcast(I32)

            def exp_parts(z, scale, em1, t):
                st.link(ts(z, z, -87.0, 88.0, ALU.max, ALU.min))
                st.link(ts(t, z, LOG2E, MAGIC, ALU.mult, ALU.add))
                st.link(ts(t, t, MAGIC, None, ALU.subtract))
                st.link(stt(z, t, -LN2_A, z, ALU.mult, ALU.add))
                st.link(stt(z, t, -LN2_B, z, ALU.mult, ALU.add))
                st.link(ts(decay_i, t, 127.0, None, ALU.add))
                st.link(ts(decay_i, decay_i, 23, None, ALU.logical_shift_left))
                st.link(nc.vector.tensor_copy(scale, decay[:, 0:GROUPS]))
                st.link(ts(em1, z, 1.0 / 5040, None, ALU.mult))
                for c in (1.0 / 720, 1.0 / 120, 1.0 / 24, 1.0 / 6, 0.5, 1.0):
                    st.link(stt(em1, em1, c, z, ALU.add, ALU.mult))

            def reduce_angle(x, t):
                st.link(ts(t, x, INV_2PI, MAGIC, ALU.mult, ALU.add))
                st.link(ts(t, t, MAGIC, None, ALU.subtract))
                for part in (PI2_A, PI2_B, PI2_C):
                    st.link(stt(x, t, -part, x, ALU.mult, ALU.add))
                st.link(ts(x, x, -PI, PI, ALU.max, ALU.min))

            scale, em1, t0, dt, mag, mag_m1, omega, ar, ai, ar_m1, t1, t2 = tmp
            exp_parts(step, scale, em1, t0)
            st.link(stt(dt, em1, 1.0, scale, ALU.add, ALU.mult))
            st.link(tt(t1, la_re, dt, ALU.mult))
            exp_parts(t1, scale, em1, t0)
            st.link(stt(mag, em1, 1.0, scale, ALU.add, ALU.mult))
            st.link(tt(em1, em1, scale, ALU.mult))
            st.link(stt(mag_m1, scale, -1.0, em1, ALU.add, ALU.add))
            st.link(tt(omega, la_im, dt, ALU.mult))
            reduce_angle(omega, t0)
            st.link(nc.vector.tensor_copy(bco[:, 0, :], omega))
            nc.vector.tensor_copy(bco[:, 1, :], omega).then_inc(sin_asked, 1)
            dve.wait_ge(sin_asked, 1)
            pairs(dve, 2, 4, u_block)
            st.link(ts(omega8[:, :], omega, float(TC), None, ALU.mult))
            reduce_angle(omega8[:, :], t0)
            st.link(ts(omega8[:, :], omega8[:, :], INV_2PI, None, ALU.mult))
            st.link(tt(mag8[:, :], mag, mag, ALU.mult))
            st.link(tt(mag8[:, :], mag8[:, :], mag8[:, :], ALU.mult))
            st.link(tt(mag8[:, :], mag8[:, :], mag8[:, :], ALU.mult))
            dve.wait_ge(sin_done, 2)
            st.link(tt(t1, bco[:, 1, :], bco[:, 1, :], ALU.mult))
            st.link(ts(t1, t1, -2.0, None, ALU.mult))
            st.link(tt(t1, t1, mag, ALU.mult))
            st.link(tt(ar_m1, t1, mag_m1, ALU.add))
            st.link(ts(ar, ar_m1, 1.0, None, ALU.add))
            st.link(tt(ai, mag, bco[:, 0, :], ALU.mult))
            st.link(tt(t0, la_re, la_re, ALU.mult))
            st.link(tt(t1, la_im, la_im, ALU.mult))
            st.link(tt(t0, t0, t1, ALU.add))
            st.link(nc.vector.reciprocal(dt, t0))
            st.link(tt(t0, ar_m1, la_re, ALU.mult))
            st.link(tt(t1, ai, la_im, ALU.mult))
            st.link(tt(t0, t0, t1, ALU.add))
            st.link(tt(bco[:, 0, :], t0, dt, ALU.mult))
            st.link(tt(t0, ai, la_re, ALU.mult))
            st.link(tt(t1, ar_m1, la_im, ALU.mult))
            st.link(tt(t0, t0, t1, ALU.subtract))
            st.link(tt(bco[:, 1, :], t0, dt, ALU.mult))
            st.link(ts(bco[:, 2, :], bco[:, 0, :], c_sgn, None, ALU.mult))
            st.link(ts(bco[:, 3, :], bco[:, 1, :], c_sgn, None, ALU.mult))
            st.link(nc.vector.memset(up_re[:, :, 0], 1.0))
            st.link(nc.vector.memset(up_im[:, :, 0], 0.0))
            st.link(nc.vector.tensor_copy(up_re[:, :, 1], ar))
            st.link(nc.vector.tensor_copy(up_im[:, :, 1], ai))
            for have in (1, 2, 4):
                lo_r, lo_i = up_re[:, :, 1:have + 1], up_im[:, :, 1:have + 1]
                by_r, by_i = (x[:, :, have:have + 1].broadcast_to([P, GROUPS, have]) for x in (up_re, up_im))
                new_r, new_i = (x[:, :, have + 1:2 * have + 1] for x in (up_re, up_im))
                wa = tA[:, 0:GROUPS * have].rearrange("p (g k) -> p g k", k=have)
                wb = tA[:, GROUPS * 4:GROUPS * (4 + have)].rearrange("p (g k) -> p g k", k=have)
                st.link(tt(wa, lo_r, by_r, ALU.mult))
                st.link(tt(wb, lo_i, by_i, ALU.mult))
                st.link(tt(new_r, wa, wb, ALU.subtract))
                st.link(tt(wa, lo_r, by_i, ALU.mult))
                st.link(tt(wb, lo_i, by_r, ALU.mult))
                st.link(tt(new_i, wa, wb, ALU.add))
            for k in range(TC):
                nc.vector.tensor_copy(dn_re[:, :, k], up_re[:, :, TC - 1 - k])
                st.mark(nc.vector.tensor_copy(dn_im[:, :, k], up_im[:, :, TC - 1 - k]))
            st.sync()
            pairs(dve, 4, 6, u_block)

            def wide(x, n):
                return x.rearrange("p (g h) -> p g h", g=GB).unsqueeze(2).broadcast_to([P, GB, n, 16])

            def params(b, j, first=False):
                dve.wait_ge(bc_loaded, b * 16 + 16)
                wait(dve, lags_done, b)
                grp = bass.ds(b * GB, GB)

                def co(i):
                    return bco[:, i, grp].unsqueeze(2).broadcast_to([P, GB, 16])

                def gh(x):
                    return x.rearrange("p (g h) -> p g h", g=GB)
                b_st, b_sw, c_st, c_sw = (gh(bcp[:, i, :]) for i in range(4))
                w0, w1, w2, w3 = (gh(bbar[:, i, :]) for i in range(4))
                st.mark(tt(w0, b_st, co(0), ALU.mult))
                st.mark(tt(w1, b_sw, co(3), ALU.mult))
                st.mark(tt(w2, b_sw, co(2), ALU.mult))
                st.link(tt(w3, b_st, co(1), ALU.mult))
                st.mark(tt(w0, w0, w1, ALU.add))
                st.link(tt(w3, w2, w3, ALU.subtract))
                st.mark(nc.vector.tensor_copy(
                    bdiag[:, :].rearrange("p (g c) -> p g c", g=GB)[:, :, 0:16], w0))
                st.mark(ts(bbar[:, 1, :], bcp[:, 2, :], c_nsgn, None, ALU.mult))
                st.link(ts(bbar[:, 2, :], bcp[:, 3, :], -1.0, None, ALU.mult))
                if not first:
                    dve.wait_ge(trig_done, b)
                x4 = tA[:, 0:GB * P].rearrange("p (g h t) -> p g h t", g=GB, h=16)

                def tall(x):
                    return gh(x).unsqueeze(3).broadcast_to([P, GB, 16, TC])

                def down(x):
                    return x[:, grp, :].unsqueeze(2).broadcast_to([P, GB, 16, TC])
                st.mark(tt(gst[:, :, :, :], tall(bbar[:, 0, :]), down(dn_re), ALU.mult))
                st.link(tt(x4, tall(bbar[:, 3, :]), down(dn_im), ALU.mult))
                st.link(tt(gst[:, :, :, :], gst[:, :, :, :], x4, ALU.add))
                wait(dve, ssm_y_done, b - 1)

                def up(x, first, n):
                    return x[:, grp, first:first + n].unsqueeze(3).broadcast_to([P, GB, n, 16])
                n9 = TC + 1
                y4 = tA[:, :].rearrange("p (g l h) -> p g l h", g=GB, l=n9)
                st.mark(tt(hc[:, j, :, :, :], wide(bbar[:, 1, :], n9), up(up_re, 0, n9), ALU.mult))
                st.link(tt(y4, wide(bbar[:, 2, :], n9), up(up_im, 0, n9), ALU.mult))
                st.link(tt(hc[:, j, :, :, :], hc[:, j, :, :, :], y4, ALU.add))
                z4 = tA[:, 0:GB * P].rearrange("p (g l h) -> p g l h", g=GB, l=TC)
                st.mark(tt(hrot[:, j, :, :, :], wide(bbar[:, 2, :], TC), up(up_re, 1, TC), ALU.mult))
                st.link(tt(z4, wide(bbar[:, 1, :], TC), up(up_im, 1, TC), ALU.mult))
                tt(hrot[:, j, :, :, :], hrot[:, j, :, :, :], z4, ALU.subtract).then_inc(params_ready, 1)
                dve.wait_ge(params_ready, b + 1)

            def phases(b, j):
                grp = bass.ds(b * GB, GB)

                def gc(x):
                    return x.rearrange("p (g c) -> p g c", g=GB)
                turns, whole = tB[:, :], tA[:, 0:T]
                st.link(tt(gc(turns), omega8[:, grp].unsqueeze(2).broadcast_to([P, GB, NC]),
                           cidx[:, :].unsqueeze(1).broadcast_to([P, GB, NC]), ALU.mult))
                st.link(ts(whole, turns, MAGIC, None, ALU.add))
                st.link(stt(turns, whole, MAGIC, turns, ALU.subtract, ALU.subtract))
                st.mark(nc.vector.tensor_copy(gc(decay[:, :]), mag8[:, grp].unsqueeze(2).broadcast_to([P, GB, NC])))
                st.sync()
                st.mark(nc.vector.memset(gc(decay[:, :])[:, :, 0:1], 0.0))
                stt(whole, turns, -1.0, turns, ALU.mult, ALU.max).then_inc(phase_ready, 1)

            def rotate_scan(b, j):
                dve.wait_ge(states_done, b + 1)
                st.mark(tt(tB[:, :], ps[:, 0, :], cos_t[:, :], ALU.mult))
                st.link(tt(tA[:, 0:T], ps[:, 1, :], sin_t[:, :], ALU.mult))
                st.link(tt(tA[:, 0:T], tA[:, 0:T], tB[:, :], ALU.add))
                st.link(nc.vector.tensor_tensor_scan(tB[:, :], decay[:, :], tA[:, 0:T], 0.0, ALU.mult, ALU.add))
                wait(dve, ssm_y_done, b)

                def part(x, first):
                    return x.rearrange("p (g c) -> p g c", g=GB)[:, :, first:first + NC - 1]
                st.mark(tt(x1[:, :, 1:NC], part(tB[:, :], 0), part(cos_t[:, :], 0), ALU.mult))
                tt(x2[:, :, 1:NC], part(tB[:, :], 0), part(sin_t[:, :], 0), ALU.mult).then_inc(rot_done, 1)

            params(0, 0, first=True)
            pairs(dve, 6, 12, u_block)

            def batch(b, j):
                if not isinstance(b, int) or b > 0:
                    rotate_scan(b - 1, 1 - j)
                    dve.wait_ge(rot_done, b)
                phases(b, j)
                if not isinstance(b, int) or b < NB - 1:
                    params(b + 1, 1 - j)
                take(N_INA + 12 + b, j, 28 + b, j)

            batch(0, 0)
            batch(1, 1)
            st.loop(2, 10, 27, batch)
            batch(10, 0)
            batch(11, 1)
            rotate_scan(11, 1)
            take(N_INA + 24, 0, 40, 0)
            take(N_INA + 25, 1, 41, 1)

            def gelu_block(i, j):
                for slot in (0, 1):
                    m = i * 2 + slot
                    dve.wait_ge(yu_loaded[slot], i * 144 + 144)
                    wait(dve, yg_done, i * 2)
                    stt(yv[:, slot, :].rearrange("p (c t) -> p t c", t=TC),
                        um[:, slot, :].rearrange("p (t c) -> p t c", t=TC), cols[:, bass.ds(C_DSKIP + m, 1)],
                        ym[:, slot, :].rearrange("p (t c) -> p t c", t=TC), ALU.mult, ALU.add).then_inc(yv_ready, 1)
                for slot in (0, 1):
                    dve.wait_ge(ysq_done, i * 2 + slot + 1)
                    st.mark(ts(yq[:, slot, :], yq[:, slot, :], 0.044715, 1.0, ALU.mult, ALU.add))
                st.sync()
                for slot in (0, 1):
                    tt(yq[:, slot, :], yq[:, slot, :], yv[:, slot, :], ALU.mult).then_inc(yin_ready, 1)
                for slot in (0, 1):
                    dve.wait_ge(yth_done, i * 2 + slot + 1)
                    stt(yv[:, slot, :], yth[:, slot, :], 1.0, yv[:, slot, :], ALU.add, ALU.mult).then_inc(yg_ready, 1)
                for slot in (0, 1):
                    m = i * 2 + slot
                    dve.wait_ge(yghi_done, m + 1)
                    stt(yg_lo[:, m, :], yv[:, slot, :], 0.5, yg_hi[:, m, :].bitcast(F32), ALU.mult,
                        ALU.subtract).then_inc(yg_done, 1)
                take(N_INA + 26 + i, j, 42 + i, j)

            dve.wait_ge(ssm_y_done, NB)
            gelu_block(0, 0)
            gelu_block(1, 1)
            st.loop(2, 6, 2, gelu_block)

            def softmax_max(u, s, widths, source):
                dve.wait_ge(scores_done, u + 1)
                wait(dve, turned, u)
                for i, w in enumerate(widths):
                    source(i, w)
                st.sync()
                for i, w in enumerate(widths):
                    last = nc.vector.tensor_reduce(nmax[:, i:i + 1], s[:, i, 0:w], AX.X, ALU.max, negate=True)
                last.then_inc(max_ready, 1)

            def softmax_scale(u, s, widths):
                dve.wait_ge(exp_done, u + 1)
                st.link(nc.vector.reciprocal(rsum[:, :], rsum[:, :]))
                for i, w in enumerate(widths):
                    last = ts(s[:, i, 0:w], s[:, i, 0:w], rsum[:, i:i + 1], None, ALU.mult)
                last.then_inc(probs_ready, 1)

            def scores_to(s, scale):
                def source(i, w):
                    st.mark(ts(s[:, i, 0:w], ps[:, i // 2, (i % 2) * NM:(i % 2) * NM + w], scale, None, ALU.mult))
                return source

            def gate_block(g, j):
                n, c = N_GLU + g, joined_main(g)
                if isinstance(g, int) and 1 <= g <= MEMH:
                    softmax_max(g - 1, s_a, [NM] * 4, scores_to(s_a, SCALE))
                    softmax_scale(g - 1, s_a, [NM] * 4)
                dve.wait_ge(act_lo_done, 32 + c)
                dve.wait_ge(tz_done, c + 1)
                dve.wait_ge(out_taken, n + 1)
                st.mark(tt(y2_a[:, :], yg_hi[:, g, :].bitcast(F32), yg_lo[:, g, :].bitcast(F32), ALU.add))
                st.link(stt(sz_a[:, :], tz_a[:, :], 1.0, z_a[:, j, :], ALU.add, ALU.mult))
                st.link(stt(y2_a[:, :], tg_a[:, :], 1.0, y2_a[:, :], ALU.add, ALU.mult))
                tt(y2_a[:, :], y2_a[:, :], sz_a[:, :], ALU.mult).then_inc(main_ready, 1)
                dve.wait_ge(main_ready, c + 1)
                low_joined(32 + c, act_lo[:, g, :], 0.25, act_hi[:, g, :])
                if isinstance(g, int) and 2 <= g <= MEMH + 1:
                    u = g - 2
                    dve.wait_ge(tz_done, c + 2)
                    st.link(stt(sz_a[:, :], tz_a[:, :], 1.0, zm_a[:, :], ALU.add, ALU.mult))
                    dve.wait_ge(att_done, u + 1)
                    dve.wait_ge(act_lo_done, 33 + c)
                    tt(y2_a[:, :], p7[:, :], sz_a[:, :], ALU.mult).then_inc(main_ready, 1)
                    dve.wait_ge(main_ready, c + 2)
                    low_joined(33 + c, act_lo[:, HEADS + u, :], 0.5, act_hi[:, HEADS + u, :])

            def low_joined(c, dst, scale, hi):
                dve.wait_ge(act_hi_done, c + 1)
                stt(dst, y2_a[:, :], scale, hi.bitcast(F32), ALU.mult, ALU.subtract).then_inc(act_lo_done, 1)

            for g in range(6):
                gate_block(g, g % 2)
            st.loop(6, 12, 3, gate_block)

            total(32, 0, acc1, sq1)
            total(33, 1, acc1, sq1)
            pairs(dve, 2, 16, lambda m, j: total(32 + m, j, acc1, sq1))
            inverse_rms(2, rbc, diag1)
            dve.wait_ge(x_loaded, 16)

            def residual(k):
                st.link(tt(o_t[:, k, :], o_t[:, k, :], rbc[:, :], ALU.mult))
                tt(h_t[:, k, :], h_t[:, k, :], o_t[:, k, :], ALU.add).then_inc(h_ready, 1)

            def h_low(k):
                low(48 + k, act_lo[:, k, :], h_t[:, k, :], cols[:, bass.ds(C_KVG + k, 1)], act_hi[:, k, :])

            def h_tile(k, j):
                st.mark(tt(o_t[:, k, :], o_t[:, k, :], rbc[:, :], ALU.mult))
                if not isinstance(k, int) or k > 1:
                    h_low(k - 2)
                st.sync()
                tt(h_t[:, k, :], h_t[:, k, :], o_t[:, k, :], ALU.add).then_inc(h_ready, 1)

            h_tile(0, 0)
            h_tile(1, 1)
            st.loop(2, 16, 1, h_tile)
            h_low(14)
            h_low(15)
            inverse_rms(3, rbc, diag1)
            pairs(dve, 0, 12, lambda m, j: take(N_KV + m, j, 48 + m, j))

            def v_block(m, j):
                wait(dve, vturned, m + 7)
                take(N_KV + 12 + m, j, None, None, vt1[:, j, :])

            pairs(dve, 0, 12, v_block)

            def again(k, j):
                low(64 + k, act_lo[:, k, :], h_t[:, k, :], cols[:, bass.ds(C_PRE + KD + k, 1)], act_hi[:, k, :])

            pairs(dve, 0, KD // 2, again)

            dve.wait_ge(gemm_done, N_FG + 1)
            dve.wait_ge(bfg_loaded, 16)
            fa, fb = fga[0:HEADS, :], fgb[0:HEADS, :]
            tt(fa, pgemm[0:HEADS, N_FG % 2, :], rbc[0:HEADS, :], ALU.mult).then_inc(out_taken, 1)
            dve.wait_ge(out_taken, N_FG + 1)
            pairs(dve, KD // 2, KD, again)

            st.link(ts(fa, fa, fq[0:HEADS, 0, 0:1], None, ALU.add))
            stt(fb, fa, -1.0, fa, ALU.mult, ALU.max).then_inc(fg_ready, 1)
            dve.wait_ge(fg_ready, 1)
            st.link(ts(fa, fa, 0.0, None, ALU.min))
            dve.wait_ge(fg_ln, 1)
            st.link(tt(fa, fa, fb, ALU.subtract))
            st.link(nc.vector.memset(fb, 1.0))
            st.link(nc.vector.tensor_tensor_scan(fb, fb, fa, 0.0, ALU.mult, ALU.add))
            ts(fb, fb, -1.0, None, ALU.mult).then_inc(fc_ready, 1)

            def q_block(m, j):
                n, slot = N_INB + m, (N_INB + j) % 2
                dve.wait_ge(gemm_done, n + 1)
                wait(dve, stage_stored[j], half(72 + m, j))
                stt(stage[:, j, :], pgemm[:, slot, :], SCALE, rbc[:, :], ALU.mult, ALU.mult).then_inc(out_taken, 1)

            q_block(0, 0)
            q_block(1, 1)
            dve.wait_ge(fq_turned, 1)
            ts(fq[:, :, :], pt[:, 0:4 * HEADS].rearrange("p (i h) -> p i h", i=4), -1.0, None,
               ALU.mult).then_inc(fq_ready, 1)
            pairs(dve, 2, 16, q_block)
            dve.wait_ge(fq_ready, 1)
            dve.wait_ge(h_stored, 16)

            fox_widths = [P, 2 * P, 3 * P, 4 * P]
            fox_out = [ps[:, 0, 0:P], p6[:, 0:2 * P], ps[:, 0, P:4 * P], ps[:, 1, :]]

            def fox_softmax(t, j):
                def source(i, w):
                    st.link(stt(s_b[:, i, 0:w], fox_out[i], fq[:, i, bass.ds(t, 1)], bias_b[:, j, 0:w],
                                ALU.add, ALU.add))
                    diag = s_b[:, i, w - P:w]
                    st.mark(tt(diag, diag, mask[:, :], ALU.add))
                softmax_max(MEMH + t, s_b, fox_widths, source)
                softmax_scale(MEMH + t, s_b, fox_widths)

            def post(t, j):
                dve.wait_ge(att_done, MEMH + t + 1)
                stt(cat_t[:, t, :], p7[:, :], 0.5, sz_b[:, j, :], ALU.mult, ALU.mult).then_inc(post_done, 1)

            def z_tile(t, j):
                take(N_INB + 16 + t, (N_INB + j) % 2, None, None, z_b[:, j, :])
                if not isinstance(t, int) or t > 0:
                    post(t - 1, 1 - j)
                dve.wait_ge(tanh_done, t + 1)
                st.link(stt(sz_b[:, j, :], sz_b[:, j, :], 1.0, z_b[:, j, :], ALU.add, ALU.mult))

            def fox_unit(t, j):
                dve.wait_ge(qk_loaded[j], half(t, j) * 3 + 48)
                fox_softmax(t, j)
                z_tile(t, j)

            fox_unit(0, 0)
            fox_unit(1, 1)
            st.loop(2, 12, 10, fox_unit)
            for t in range(HEADS, UNITS):
                softmax_max(MEMH + t, s_b, [NM] * 4, scores_to(s_b, 1.0))
                softmax_scale(MEMH + t, s_b, [NM] * 4)
                z_tile(t, t % 2)
            post(15, 1)

            def cat_tile(k, j):
                low(80 + k, act_lo[:, k, :], cat_t[:, k, :], None, act_hi[:, k, :])

            dve.wait_ge(post_done, UNITS)
            pairs(dve, 0, 16, cat_tile)
            total(64, 0, acc1, sq1)
            total(65, 1, acc1, sq1)
            pairs(dve, 2, 16, lambda m, j: total(64 + m, j, acc1, sq1))
            inverse_rms(4, rbc, diag1)
            dve.wait_ge(h_loaded, 16)
            st.loop(0, TAIL, 1, lambda k, j: residual(k))


def kernel(x, mem, pre_norm_g, post_norm_g, w_in_a, lam_re, lam_im, log_step, b_re, b_im, c_re, c_im, d_skip,
           w_glu, b_glu, kv_norm_g, w_kv, w_fgate, b_fgate, w_in_b, mem_norm_g, w_mem_kv, w_out):
    import numpy as np
    import concourse.bacc as bacc
    from concourse.bass_utils import run_bass_kernel_spmd

    def tiles(a):
        return a.T.reshape(-1, P, a.shape[0])

    def blocks(w):
        k, m = w.shape
        return w.reshape(k // P, P, m // P, P).transpose(2, 1, 0, 3).reshape(m // P, P, -1)

    def columns(g):
        return g.reshape(-1, P).T

    def twice(a):
        return np.concatenate([a.T, a.T])

    def batches(top, bottom):
        a = np.concatenate([top, bottom], axis=1).reshape(NB, GB, P, 16)
        return a.transpose(0, 2, 1, 3).reshape(NB, P, P)

    cols = np.concatenate([columns(g) for g in (pre_norm_g, post_norm_g, kv_norm_g, mem_norm_g, b_glu, d_skip)], axis=1)
    steps = np.broadcast_to(log_step[0][None, :], (P, GROUPS))
    c_r, c_i = c_re[0].transpose(0, 2, 1), c_im[0].transpose(0, 2, 1)
    fg = np.zeros((D, P), w_fgate.dtype)
    fg[:, :HEADS] = w_fgate
    b_blocks = blocks(w_in_b[0])
    ins = {
        "x_t": tiles(x[0]), "mem_t": tiles(mem[0]), "cols_d": cols, "bfg_d": b_fgate.reshape(HEADS, 1),
        "lam_d": np.concatenate([twice(lam_re[0]), twice(lam_im[0]), steps], axis=1),
        "bc_d": np.stack([batches(b_re[0], b_im[0]), batches(b_im[0], b_re[0]), batches(c_r, c_i),
                          batches(c_i, c_r)], axis=2),
        "w_mem": np.concatenate([blocks(w_mem_kv[0]), blocks(w_mem_kv[1])]), "w_in_a": blocks(w_in_a[0]),
        "w_glu": blocks(w_glu[0]), "w_out": np.stack([blocks(w_out[0]), blocks(w_out[1])]), "w_kv": blocks(w_kv),
        "w_fg": blocks(fg),
        "w_in_b": np.concatenate([b_blocks[0:12], b_blocks[24:28], b_blocks[12:24], b_blocks[28:32]]),
    }
    nc = bacc.Bacc("TRN2", target_bir_lowering=False, num_devices=1)
    arrays = {name: np.ascontiguousarray(a) for name, a in ins.items()}
    args = [nc.dram_tensor(name, a.shape, mybir.dt.from_np(a.dtype), kind="ExternalInput").ap()
            for name, a in arrays.items()]
    out = nc.dram_tensor("out_t", (KD, P, T), F32, kind="ExternalOutput").ap()
    trunk(nc, *args, out)
    r = run_bass_kernel_spmd(nc, [arrays], core_ids=[0])
    return r.results[0]["out_t"].reshape(D, T).T[None]
```
